# Optimizing a Trainium2 kernel written in Bass

```python
import math
import jax, jax.numpy as jnp
from jax import lax
import numpy as np

D_MODEL = 1024
BATCH = 1
SEQ = 256
DEPTH = 2

N_META = 16
D_FF = 2816
NORM_EPS = 1e-6

RET_HEADS = 4
RET_DK = 128
RET_DV = 128
RET_CHUNK = 128
GDN_HEADS = 4
GDN_DK = 128
GDN_DV = 128
GDN_CONV = 4
GDN_CHUNK = 64
GDN_QKV = 2 * GDN_HEADS * GDN_DK + GDN_HEADS * GDN_DV
SWA_HEADS = 8
SWA_KV_HEADS = 2
SWA_DH = 64
SWA_WINDOW = 128
SB_HEADS = 8
SB_DH = 64
ATT_BLOCK = 128

AB_WIDTHS = (RET_HEADS * RET_DK, RET_HEADS * RET_DK, RET_HEADS * RET_DV, RET_HEADS * RET_DV,
             GDN_QKV, GDN_HEADS * GDN_DV, GDN_HEADS, GDN_HEADS)
AB_IN = 2 * RET_HEADS * RET_DK + 2 * RET_HEADS * RET_DV + GDN_QKV + GDN_HEADS * GDN_DV + 2 * GDN_HEADS
AB_OUT = RET_HEADS * RET_DV + GDN_HEADS * GDN_DV
CD_WIDTHS = (SWA_HEADS * SWA_DH, SWA_KV_HEADS * SWA_DH, SWA_KV_HEADS * SWA_DH,
             SB_HEADS * SB_DH, SB_HEADS * SB_DH, SB_HEADS * SB_DH)
CD_IN = SWA_HEADS * SWA_DH + 2 * SWA_KV_HEADS * SWA_DH + 3 * SB_HEADS * SB_DH
CD_OUT = SWA_HEADS * SWA_DH + SB_HEADS * SB_DH

kernel_name = "hybrid_retention_gdn_swa_stickbreak_macaron"

def rms_norm(x, g):
    xf = x.astype(jnp.float32)
    y = xf * lax.rsqrt(jnp.mean(xf * xf, axis=-1, keepdims=True) + NORM_EPS)
    return (y * g.astype(jnp.float32)).astype(x.dtype)

def l2_normalize(x):
    return x * lax.rsqrt(jnp.sum(x * x, axis=-1, keepdims=True) + NORM_EPS)

def swiglu(x, w_gate, w_up, w_down):
    return (jax.nn.silu(x @ w_gate) * (x @ w_up)) @ w_down

def split_cols(t, widths):
    return jnp.split(t, np.cumsum(widths)[:-1].tolist(), axis=-1)

def pad_front(t, n):
    return jnp.pad(t, [(0, 0), (n, 0)] + [(0, 0)] * (t.ndim - 2))

def rotate_pairs(x, pos):
    d = x.shape[-1]
    inv_freq = 1.0 / (10000.0 ** jnp.linspace(0.0, 1.0, d // 2, dtype=jnp.float32))
    ang = pos[:, None] * inv_freq[None, :]
    cos = jnp.cos(ang)[None, :, None, :]
    sin = jnp.sin(ang)[None, :, None, :]
    x1, x2 = x[..., 0::2], x[..., 1::2]
    return jnp.stack([x1 * cos - x2 * sin, x2 * cos + x1 * sin], axis=-1).reshape(x.shape)

def causal_depthwise_conv(x, w):
    K, ch = w.shape
    return lax.conv_general_dilated(x, w[:, None, :], window_strides=(1,), padding=[(K - 1, 0)],
                                    dimension_numbers=('NWC', 'WIO', 'NWC'), feature_group_count=ch)

def retention_chunked(q, k, v):
    B, Lp, H, dk = q.shape
    dv = v.shape[-1]
    C = RET_CHUNK
    N = Lp // C
    q = q.reshape(B, N, C, H, dk)
    k = k.reshape(B, N, C, H, dk)
    v = v.reshape(B, N, C, H, dv)
    log_gamma = jnp.log1p(-jnp.exp2(-5.0 - jnp.arange(H, dtype=jnp.float32)))
    idx = jnp.arange(C, dtype=jnp.float32)
    diff = idx[:, None] - idx[None, :]
    intra_decay = jnp.where(diff >= 0, jnp.exp(jnp.maximum(diff, 0.0) * log_gamma[:, None, None]), 0.0)
    scores = jnp.einsum('bnihd,bnjhd->bnhij', q, k) * intra_decay
    intra = jnp.einsum('bnhij,bnjhe->bnihe', scores, v)
    zeta = jnp.exp((C - 1.0 - idx)[:, None] * log_gamma[None, :])
    xi = jnp.exp((idx + 1.0)[:, None] * log_gamma[None, :])
    kv = jnp.einsum('bnjhd,bnjhe->bnhde', k * zeta[..., None], v)
    chunk_decay = jnp.exp(C * log_gamma)[:, None, None]

    def step(S, kv_n):
        return S * chunk_decay + kv_n, S

    _, s_prev = lax.scan(step, jnp.zeros_like(kv[:, 0]), jnp.moveaxis(kv, 1, 0))
    s_prev = jnp.moveaxis(s_prev, 0, 1)
    cross = jnp.einsum('bnihd,bnhde->bnihe', q * xi[..., None], s_prev)
    return (intra + cross).reshape(B, Lp, H, dv)

def gated_delta_chunked(q, k, v, g, beta):
    B, Lp, H, dk = q.shape
    dv = v.shape[-1]
    C = GDN_CHUNK
    N = Lp // C

    def chunks(t):
        return jnp.moveaxis(t.reshape((B, N, C, H) + t.shape[3:]), 2, 3)

    q = chunks(q) * dk ** -0.5
    k = chunks(k)
    v = chunks(v)
    g = chunks(g)
    beta = chunks(beta)
    g_cum = jnp.cumsum(g, axis=-1)
    idx = jnp.arange(C)
    incl = idx[:, None] >= idx[None, :]
    strict = idx[:, None] > idx[None, :]
    gdiff = g_cum[..., :, None] - g_cum[..., None, :]
    decay = jnp.where(incl, jnp.exp(jnp.where(incl, gdiff, 0.0)), 0.0)
    k_beta = k * beta[..., None]
    a_mat = jnp.where(strict, jnp.einsum('bnhid,bnhjd->bnhij', k_beta, k) * decay, 0.0)
    system = a_mat + jnp.eye(C, dtype=a_mat.dtype)
    rhs = jnp.concatenate([v * beta[..., None], k_beta * jnp.exp(g_cum)[..., None]], axis=-1)
    sol = lax.linalg.triangular_solve(system, rhs, left_side=True, lower=True, unit_diagonal=True)
    u_vec, w_vec = sol[..., :dv], sol[..., dv:]
    qk = jnp.where(incl, jnp.einsum('bnhid,bnhjd->bnhij', q, k) * decay, 0.0)
    q_dec = q * jnp.exp(g_cum)[..., None]
    g_last = g_cum[..., -1]
    k_tail = k * jnp.exp(g_last[..., None] - g_cum)[..., None]

    def step(S, xs):
        u_n, w_n, qk_n, qd_n, kt_n, gl_n = xs
        v_new = u_n - jnp.einsum('bhcd,bhde->bhce', w_n, S)
        o_n = jnp.einsum('bhcd,bhde->bhce', qd_n, S) + jnp.einsum('bhij,bhje->bhie', qk_n, v_new)
        S = S * jnp.exp(gl_n)[..., None, None] + jnp.einsum('bhcd,bhce->bhde', kt_n, v_new)
        return S, o_n

    xs = tuple(jnp.moveaxis(t, 1, 0) for t in (u_vec, w_vec, qk, q_dec, k_tail, g_last))
    _, o = lax.scan(step, jnp.zeros((B, H, dk, dv), q.dtype), xs)
    return jnp.moveaxis(o, 0, 1).transpose(0, 1, 3, 2, 4).reshape(B, Lp, H, dv)

def swa_sink_attention(q, k, v, sinks):
    B, Lp, HQ, dh = q.shape
    HKV = k.shape[2]
    G = HQ // HKV
    BLK = ATT_BLOCK
    NB = Lp // BLK
    pad = BLK - N_META
    qb = q.reshape(B, NB, BLK, HKV, G, dh) * dh ** -0.5
    kb = k.reshape(B, NB, BLK, HKV, dh)
    vb = v.reshape(B, NB, BLK, HKV, dh)
    shift = ((0, 0), (1, 0), (0, 0), (0, 0), (0, 0))
    k_prev = jnp.pad(kb, shift)[:, :-1]
    v_prev = jnp.pad(vb, shift)[:, :-1]
    meta_k = jnp.broadcast_to(k[:, None, pad:BLK], (B, NB, N_META, HKV, dh))
    meta_v = jnp.broadcast_to(v[:, None, pad:BLK], (B, NB, N_META, HKV, dh))
    keys = jnp.concatenate([meta_k, k_prev, kb], axis=2)
    vals = jnp.concatenate([meta_v, v_prev, vb], axis=2)
    blocks = jnp.arange(NB)
    qpos = blocks[:, None] * BLK + jnp.arange(BLK)[None, :]
    kpos = (blocks[:, None] - 1) * BLK + jnp.arange(2 * BLK)[None, :]
    dpos = qpos[:, :, None] - kpos[:, None, :]
    band = (dpos >= 0) & (dpos < SWA_WINDOW) & (kpos[:, None, :] >= BLK)
    meta_vis = (pad + jnp.arange(N_META))[None, None, :] <= qpos[:, :, None]
    mask = jnp.concatenate([jnp.broadcast_to(meta_vis, (NB, BLK, N_META)), band], axis=-1)
    s = jnp.einsum('bnqhgd,bnkhd->bnhgqk', qb, keys)
    s = jnp.where(mask[None, :, None, None], s, -jnp.inf)
    sink = jnp.broadcast_to(sinks.astype(s.dtype).reshape(1, 1, HKV, G, 1, 1), s.shape[:-1] + (1,))
    p = jax.nn.softmax(jnp.concatenate([s, sink], axis=-1), axis=-1)[..., :-1]
    o = jnp.einsum('bnhgqk,bnkhd->bnqhgd', p, vals)
    return o.reshape(B, Lp, HQ, dh)

def stick_breaking_attention(q, k, v):
    B, Lp, H, dh = q.shape
    BLK = ATT_BLOCK
    NB = Lp // BLK
    pad = BLK - N_META
    kpos = jnp.arange(Lp)
    qb = jnp.moveaxis(q.reshape(B, NB, BLK, H, dh), 1, 0)
    scale = dh ** -0.5

    def block(args):
        q_blk, n = args
        qpos = n * BLK + jnp.arange(BLK)
        valid = (kpos[None, :] < qpos[:, None]) & (kpos[None, :] >= pad)
        z = jnp.einsum('bqhd,bkhd->bhqk', q_blk, k) * scale
        log_beta = jax.nn.log_sigmoid(z)
        log_1m_beta = jnp.where(valid, jax.nn.log_sigmoid(-z), 0.0)
        log_stick = lax.cumsum(log_1m_beta, axis=3, reverse=True) - log_1m_beta
        a = jnp.where(valid, jnp.exp(log_beta + log_stick), 0.0)
        return jnp.einsum('bhqk,bkhd->bqhd', a, v)

    o = lax.map(block, (qb, jnp.arange(NB)))
    return jnp.moveaxis(o, 0, 1).reshape(B, Lp, H, dh)

def mixer_ab(u, w_in, conv_w, a_log, dt_bias, out_norm, w_out):
    B, L, _ = u.shape
    f32 = jnp.float32
    rq, rk, rv, rg, gqkv, gz, gb, ga = split_cols(u @ w_in, AB_WIDTHS)
    pos = jnp.arange(L, dtype=f32)
    rq = rotate_pairs(rq.astype(f32).reshape(B, L, RET_HEADS, RET_DK), pos)
    rk = rotate_pairs(rk.astype(f32).reshape(B, L, RET_HEADS, RET_DK), pos) * RET_DK ** -0.5
    rv = rv.astype(f32).reshape(B, L, RET_HEADS, RET_DV)
    rpad = RET_CHUNK - N_META
    ret = retention_chunked(pad_front(rq, rpad), pad_front(rk, rpad), pad_front(rv, rpad))[:, rpad:]
    mu = jnp.mean(ret, axis=-1, keepdims=True)
    var = jnp.mean(jnp.square(ret - mu), axis=-1, keepdims=True)
    ret = ((ret - mu) * lax.rsqrt(var + NORM_EPS)).reshape(B, L, -1) * jax.nn.silu(rg.astype(f32))
    qkv = jax.nn.silu(causal_depthwise_conv(gqkv.astype(f32), conv_w.astype(f32)))
    gq, gk, gv = split_cols(qkv, (GDN_HEADS * GDN_DK, GDN_HEADS * GDN_DK, GDN_HEADS * GDN_DV))
    gq = l2_normalize(gq.reshape(B, L, GDN_HEADS, GDN_DK))
    gk = l2_normalize(gk.reshape(B, L, GDN_HEADS, GDN_DK))
    gv = gv.reshape(B, L, GDN_HEADS, GDN_DV)
    beta = jax.nn.sigmoid(gb.astype(f32))
    g = -jnp.exp(a_log.astype(f32)) * jax.nn.softplus(ga.astype(f32) + dt_bias.astype(f32))
    gpad = GDN_CHUNK - N_META
    o = gated_delta_chunked(*(pad_front(t, gpad) for t in (gq, gk, gv, g, beta)))[:, gpad:]
    o = rms_norm(o, out_norm) * jax.nn.silu(gz.astype(f32).reshape(B, L, GDN_HEADS, GDN_DV))
    mixed = jnp.concatenate([ret, o.reshape(B, L, -1)], axis=-1).astype(u.dtype)
    return mixed @ w_out

def mixer_cd(u, w_in, sinks, w_out):
    B, L, _ = u.shape
    pad = ATT_BLOCK - N_META
    Lp = L + pad
    cq, ck, cv, sq, sk, sv = [pad_front(t.astype(jnp.float32), pad) for t in split_cols(u @ w_in, CD_WIDTHS)]
    swa = swa_sink_attention(cq.reshape(B, Lp, SWA_HEADS, SWA_DH), ck.reshape(B, Lp, SWA_KV_HEADS, SWA_DH),
                             cv.reshape(B, Lp, SWA_KV_HEADS, SWA_DH), sinks)
    sb = stick_breaking_attention(sq.reshape(B, Lp, SB_HEADS, SB_DH), sk.reshape(B, Lp, SB_HEADS, SB_DH),
                                  sv.reshape(B, Lp, SB_HEADS, SB_DH))
    mixed = jnp.concatenate([swa.reshape(B, Lp, -1), sb.reshape(B, Lp, -1)], axis=-1)[:, pad:]
    return mixed.astype(u.dtype) @ w_out

def setup_inputs(seed: int = 0) -> dict:
    key = jax.random.key(seed)
    ks = jax.random.split(key, 16)
    f32 = jnp.float32
    n_even = (DEPTH + 1) // 2
    n_odd = DEPTH // 2

    def dense(k, shape, fan_in):
        return jax.random.normal(k, shape, f32) * fan_in ** -0.5

    x = jax.random.normal(ks[0], (BATCH, SEQ, D_MODEL), f32)
    meta_tokens = jax.random.normal(ks[1], (N_META, D_MODEL), f32)
    norm_gains = 1.0 + 0.01 * jax.random.normal(ks[2], (DEPTH, 6, D_MODEL), f32)
    ffn_w_gate = dense(ks[3], (DEPTH, 2, D_MODEL, D_FF), D_MODEL)
    ffn_w_up = dense(ks[4], (DEPTH, 2, D_MODEL, D_FF), D_MODEL)
    ffn_w_down = dense(ks[5], (DEPTH, 2, D_FF, D_MODEL), D_FF)
    ab_w_in = dense(ks[6], (n_even, D_MODEL, AB_IN), D_MODEL)
    ab_conv_w = dense(ks[7], (n_even, GDN_CONV, GDN_QKV), GDN_CONV)
    ab_a_log = jnp.log(jax.random.uniform(ks[8], (n_even, GDN_HEADS), f32, 1.0, 16.0))
    dt = jnp.exp(jax.random.uniform(ks[9], (n_even, GDN_HEADS), f32, math.log(1e-3), math.log(1e-1)))
    ab_dt_bias = dt + jnp.log(-jnp.expm1(-dt))
    ab_out_norm = 1.0 + 0.01 * jax.random.normal(ks[10], (n_even, GDN_DV), f32)
    ab_w_out = dense(ks[11], (n_even, AB_OUT, D_MODEL), AB_OUT)
    cd_w_in = dense(ks[12], (n_odd, D_MODEL, CD_IN), D_MODEL)
    cd_sinks = jax.random.normal(ks[13], (n_odd, SWA_HEADS), f32)
    cd_w_out = dense(ks[14], (n_odd, CD_OUT, D_MODEL), CD_OUT)
    return {"x": x, "meta_tokens": meta_tokens, "norm_gains": norm_gains,
            "ffn_w_gate": ffn_w_gate, "ffn_w_up": ffn_w_up, "ffn_w_down": ffn_w_down,
            "ab_w_in": ab_w_in, "ab_conv_w": ab_conv_w, "ab_a_log": ab_a_log, "ab_dt_bias": ab_dt_bias,
            "ab_out_norm": ab_out_norm, "ab_w_out": ab_w_out,
            "cd_w_in": cd_w_in, "cd_sinks": cd_sinks, "cd_w_out": cd_w_out}

def reference(x, meta_tokens, norm_gains, ffn_w_gate, ffn_w_up, ffn_w_down,
              ab_w_in, ab_conv_w, ab_a_log, ab_dt_bias, ab_out_norm, ab_w_out,
              cd_w_in, cd_sinks, cd_w_out):
    B = x.shape[0]
    meta = jnp.broadcast_to(meta_tokens[None].astype(x.dtype), (B, N_META, D_MODEL))
    h = jnp.concatenate([meta, x], axis=1)
    for i in range(DEPTH):
        g = norm_gains[i]
        j = i // 2
        y = swiglu(rms_norm(h, g[0]), ffn_w_gate[i, 0], ffn_w_up[i, 0], ffn_w_down[i, 0])
        h = h + 0.5 * rms_norm(y, g[1])
        u = rms_norm(h, g[2])
        if i % 2 == 0:
            y = mixer_ab(u, ab_w_in[j], ab_conv_w[j], ab_a_log[j], ab_dt_bias[j], ab_out_norm[j], ab_w_out[j])
        else:
            y = mixer_cd(u, cd_w_in[j], cd_sinks[j], cd_w_out[j])
        h = h + rms_norm(y, g[3])
        y = swiglu(rms_norm(h, g[4]), ffn_w_gate[i, 1], ffn_w_up[i, 1], ffn_w_down[i, 1])
        h = h + 0.5 * rms_norm(y, g[5])
    return h[:, N_META:]


_drawn_inputs = setup_inputs


def setup_inputs(seed=0):
    import zlib

    import numpy as np

    out = dict(_drawn_inputs(seed))
    spreads = {}
    factors = {'ab_out_norm': 8.0, 'cd_sinks': 8.0}
    for name, (base, spread) in spreads.items():
        noise = np.random.default_rng([zlib.crc32(name.encode()), seed]).standard_normal(out[name].shape)
        drawn = base * np.exp(spread * noise) if base else spread * noise
        out[name] = __import__('jax').numpy.asarray(drawn.astype(out[name].dtype))
    for name, factor in factors.items():
        out[name] = (out[name] * factor).astype(out[name].dtype)
    return out
```

```python
from contextlib import ExitStack

import concourse.bass as bass
from concourse import mybir
import numpy as np
F32 = mybir.dt.float32
F32R = mybir.dt.float32r
ALU = mybir.AluOpType
ACT = mybir.ActivationFunctionType
AX = mybir.AxisListType

P = 128
N_META = 16
SEQ = 256
T = N_META + SEQ
D = 1024
KD = D // P
FF = 2816
KF = FF // P
EPS = 1e-6
CB = 256
KH = KF // 2
RAW = KH * CB
NRAW = 4
NW = 2
NPAIR = FF // CB
NBLK = D // CB
BANK = 512
LN_HALF = float(np.log(0.5))
LN_QSCALE = float(-0.5 * np.log(128.0))

EXP_SET = "natural_log_exp_and_others"
SILU_SET = "silu_and_others"

AB_IN = 4104
CD_IN = 2304
AB_CHUNKS = AB_IN // CB
CD_CHUNKS = CD_IN // CB

SUBLAYERS = [("ffn", 0), ("ab", 0), ("ffn", 0), ("ffn", 1), ("cd", 1), ("ffn", 1)]
SIZES = {"ffn": 2 * NPAIR + 2 * NBLK, "ab": AB_CHUNKS + NBLK, "cd": CD_CHUNKS + NBLK}

HR = HG = 4
TAIL = 32
TP = 2 * P + TAIL
N_MASKS = 8
UPPER, UPPER32, LOWER, LOWER32, DIAG16, MERGE = 0, 1, 2, 3, 4, 5
TOK = [(0, P), (P, P), (2 * P, T - 2 * P)]

AB_ORDER = [2048 + CB * n for n in range(6)] + [1536, 1792, 3584, 3840] + [CB * n for n in range(6)]
AB_CONV, AB_GATES, AB_ROT, AB_V = range(0, 6), range(6, 10), range(10, 14), range(14, 16)

HS, DH = 8, 64
WINDOW = 128
NEG = -1e30
SB_TILES = [(0, 0), (P, P), (T - P, 2 * P)]
SBW = sum(T - q0 for _, q0 in SB_TILES)

HS, DH = 8, 64
WINDOW = 128
NEG = -1e30
SB_TILES = [(0, 0), (P, P), (T - P, 2 * P)]
SBW = sum(T - q0 for _, q0 in SB_TILES)

HS, DH = 8, 64
WINDOW = 128
NEG = -1e30
SB_TILES = [(0, 0), (P, P), (T - P, 2 * P)]
SBW = sum(T - q0 for _, q0 in SB_TILES)


def shape_constants():
    c = {}
    c["c_ident"] = np.eye(P, dtype=np.float32)
    i, j = np.arange(P)[:, None], np.arange(P)[None, :]
    masks = np.zeros((P, N_MASKS, P), np.float32)
    masks[:, UPPER] = i <= j
    masks[:, UPPER32] = (i <= j) & (i // TAIL == j // TAIL)
    masks[:, LOWER] = i > j
    masks[:, LOWER32] = (i > j) & (i // TAIL == j // TAIL)
    masks[:, DIAG16] = -1.0 * (i // 16 == j // 16)
    for n, size in enumerate((16, 32, 64)):
        masks[:, MERGE + n] = (i // (2 * size) == j // (2 * size)) & (j // size == i // size + 1)
    c["c_masks"] = masks
    swap = np.zeros((P, P), np.float32)
    swap[np.arange(1, P, 2), np.arange(0, P, 2)] = -1.0
    swap[np.arange(0, P, 2), np.arange(1, P, 2)] = 1.0
    c["c_swap"] = swap
    inv_freq = (1.0 / (np.float32(10000.0) ** np.linspace(0.0, 1.0, P // 2, dtype=np.float32))).astype(np.float32)
    ang = np.repeat(inv_freq, 2)[:, None] * np.arange(T, dtype=np.float32)[None, :]
    c["c_rope"] = np.stack([np.cos(ang), np.sin(ang)], axis=1).astype(np.float32)
    gamma = np.log1p(-np.exp2(-5.0 - np.arange(HR, dtype=np.float64)))[None, :, None]
    diff = (np.arange(T)[None, None, :] - np.arange(P)[:, None, None]).astype(np.float64)
    c["c_decay"] = (np.where(diff >= 0, np.exp(np.maximum(diff, 0) * gamma), 0.0) * P ** -0.5).astype(np.float32)
    key, q = np.arange(T)[None, None, :], np.arange(P)[:, None, None] + P * np.arange(3)[None, :, None]
    q = np.where(q < 2 * P, q, 2 * P + q % TAIL)
    sees = (key <= q) & ((key < N_META) | (q - key < WINDOW)) | (q >= T)
    c["c_window"] = np.where(sees, 0.0, NEG).astype(np.float32)
    c["c_before"] = np.concatenate([(k0 + np.arange(P)[:, None] < np.arange(q0, T)[None, :])
                                    & (k0 + np.arange(P)[:, None] >= q0) for k0, q0 in SB_TILES], axis=1).astype(np.float32)
    c["c_head_of"] = (i[:, 0:1] // TAIL == np.arange(HG)[None, :]).astype(np.float32)
    return c


class Steps:

    def __init__(self, engine, sem):
        self.engine, self.sem, self.n, self.loop = engine, sem, 0, 0

    def done(self, ins):
        ins.then_inc(self.sem, 1)
        self.n += 1
        self.engine.wait_ge(self.sem, self.n + self.loop)

    def enter(self, i, steps):
        self.loop, self.until = i * steps, self.n + steps

    def leave(self, steps, count):
        assert self.n == self.until
        self.n += steps * (count - 1)
        self.loop = 0


def build(nc, a, c, out):
    ctx = ExitStack()
    place = [nc.sbuf_base + (-nc.sbuf_base) % 64]

    def at(name, shape, dtype, where):
        return nc.alloc_sbuf_tensor_at(name, shape, dtype, offset=where)

    def sb(name, free, dtype=F32, parts=P):
        size = 4
        for n in free:
            size *= n
        t = at(name, [parts, *free], dtype, place[0])
        place[0] += size + (-size) % 64
        return t

    def sem(name):
        return ctx.enter_context(nc.semaphore(name))

    with ctx:
        raw = sb("raw", [NRAW, RAW])
        w_hi = sb("w_hi", [NW, RAW], F32R)
        w_lo = sb("w_lo", [NW, RAW], F32R)
        hT = sb("hT", [KD, T])
        yT = sb("yT", [KD, T])
        u_hi = sb("u_hi", [KD, T], F32R)
        u_lo = sb("u_lo", [KD, T], F32R)
        ss = sb("ss", [T])
        lnv = sb("lnv", [T])
        rstd = sb("rstd", [2, T])
        ident = sb("ident", [P])
        ones = sb("ones", [P])
        gains = sb("gains", [12 * KD])
        masks = sb("masks", [N_MASKS, P])
        swap = sb("swap", [P])
        head_of = sb("head_of", [HG])
        convw = sb("convw", [4 * 12])
        w_ba = sb("w_ba", [KD, 2 * HG])
        dt4 = sb("dt4", [HG])
        alog4 = sb("alog4", [HG])
        out_norm = sb("out_norm", [1])
        scratch = place[0]
        gates = sb("gates", [2, 2, T])
        prod = sb("prod", [2, 2, T])
        y_sq = sb("y_sq", [2, 2, T])
        h_sq = sb("h_sq", [2, 2, T])
        arena = place[0]
        hid_hi = at("hid_hi", [P, KF, T], F32R, arena)
        hid_lo = at("hid_lo", [P, KF, T], F32R, arena + KF * T * 4)
        x_tok = at("x_tok", [P, 3, D], F32, arena)
        g_tok = at("g_tok", [12 * KD, P], F32, arena + 3 * D * 4)
        o_tok = at("o_tok", [P, 2, D], F32, arena)
        cw_tok = at("cw_tok", [4 * 12, P], F32, arena + 3 * D * 4 + P * 4)
        assert arena + 2 * KF * T * 4 <= nc.sbuf_usable_end

        place[0] = scratch
        gq = sb("gq", [HG, TP])
        gk = sb("gk", [HG, TP])
        gv = sb("gv", [HG, TP])
        gz = sb("gz", [HG, T])
        ba = sb("ba", [3, 2 * HG])
        beta9 = sb("beta9", [9])
        g9 = sb("g9", [9])
        gc9 = sb("gc9", [9])
        small = sb("small", [8, 3 * HG])
        r9 = sb("r9", [9])
        gdn_place = place[0]
        rope = sb("rope", [2, T])
        decay = sb("decay", [HR, T])
        rq = sb("rq", [HR, T])
        rk = sb("rk", [HR, T])
        rv = sb("rv", [HR, T])
        rg = sb("rg", [HR, T])
        cacc = sb("cacc", [2, 2, T])
        qraw = sb("qraw", [2, T])
        rot = sb("rot", [2, T])
        l2sq = sb("l2sq", [2, TP])
        l2r = sb("l2r", [2, TP])
        rv_tok = sb("rv_tok", [3, HR * P])
        attn = sb("attn", [HR, T + T - P + 16])
        ret = sb("ret", [HR, T])
        assert place[0] <= nc.sbuf_usable_end
        place[0] = gdn_place
        dmat = sb("dmat", [9, P])
        dT = sb("dT", [9, P])
        dN = sb("dN", [9, P])
        eG = sb("eG", [9, P])
        PP = sb("PP", [2, 9, P])
        XX = sb("XX", [2, 9, P])
        R = sb("R", [9, P])
        ktail = sb("ktail", [8, P])
        vnew = sb("vnew", [HG, P])
        S = sb("S", [HG, P])
        vtmp = sb("vtmp", [HG, P])
        assert place[0] <= nc.sbuf_usable_end
        off_diag = eG
        w1 = dN
        O = gv[:, :, :].rearrange("p h t -> p (h t)").rearrange("p (n c) -> p n c", c=P)

        place[0] = scratch
        sbq = sb("sbq", [HS // 2, T])
        sbk = sb("sbk", [HS // 2, T])
        sbv = sb("sbv", [HS // 2, T])
        cq = sb("cq", [HS // 2, TP])
        kdup = sb("kdup", [2, T])
        cv = sb("cv", [T])
        window = sb("window", [3, T])
        before = sb("before", [SBW])
        sinks8 = sb("sinks8", [2, HS])
        sinks2 = sb("sinks2", [2])
        cv_tok = sb("cv_tok", [3, P])
        sbv_tok = sb("sbv_tok", [3, HS * DH])
        probs = sb("probs", [2, 4 * TP])
        probsT = sb("probsT", [8, P])
        wmx = sb("wmx", [2, 4, 8])
        zs = sb("zs", [4, SBW])
        sp1 = sb("sp1", [4, SBW])
        lb = sb("lb", [4, SBW])
        lm = sb("lm", [4, SBW])
        assert place[0] <= nc.sbuf_usable_end

        ps = ctx.enter_context(nc.psum_tensor("ps", [P, 8, BANK], F32))

        s_in = sem("inputs_loaded")
        s_const = sem("constants_loaded")
        s_ones = sem("ones_set")
        s_gT = sem("gains_transposed")
        s_gains = sem("gains_ready")
        s_xT = sem("input_transposed")
        s_raw = [sem(f"raw_loaded_{i}") for i in range(NRAW)]
        s_hi = sem("hi_split")
        s_lo = sem("lo_split")
        s_used = sem("chunk_used")
        s_silu = sem("silu_ready")
        s_hid = sem("hidden_ready")
        s_ysq = sem("y_squared")
        s_ss = sem("y_squares_added")
        s_ysum = sem("y_sum_ready")
        s_h = sem("h_group_ready")
        s_hsq = sem("h_squared")
        s_hsum = sem("h_squares_summed")
        s_rstd = sem("rstd_ready")
        s_u32 = sem("u32_ready")
        s_uhi = sem("u_hi_ready")
        s_ulo = sem("u_lo_ready")
        s_act = sem("act_step")
        s_dve = sem("dve_step")
        s_oT = sem("output_transposed")
        s_oc = sem("output_copied")
        s_out = sem("output_stored")

        s_cwT = sem("conv_weights_transposed")
        s_cwc = sem("conv_weights_copied")
        s_tab = sem("ab_tables_loaded")
        s_pads = sem("ab_pads_zeroed")
        s_ba = sem("ba_projected")
        s_bac = sem("ba_copied")
        s_conv = sem("conv_done")
        s_csilu = sem("conv_silu_done")
        s_evac = sem("ab_chunk_copied")
        s_swap = sem("pairs_swapped")
        s_rot = sem("rotated")
        s_l2sq = sem("l2_squared")
        s_l2sum = sem("l2_summed")
        s_l2r = sem("l2_root_ready")
        s_l2 = sem("l2_normed")
        s_rvT = sem("ret_v_transposed")
        s_rvc = sem("ret_v_copied")
        s_score = sem("ret_scores")
        s_attn = sem("ret_scores_decayed")
        s_pv = sem("ret_out")
        s_ret = sem("ret_out_copied")
        s_mean = sem("ret_mean")
        s_cent = sem("ret_centered")
        s_rsq = sem("ret_squared")
        s_var = sem("ret_var")
        s_rrt = sem("ret_root_ready")
        s_m32 = sem("mixed32_ready")
        s_mhi = sem("mixed_hi_ready")
        s_mlo = sem("mixed_lo_ready")
        s_x = sem("decay_input_ready")
        s_xe = sem("decay_exps_ready")
        s_g9 = sem("g_beta_ready")
        s_gsum = sem("g_cumulated")
        s_dcl = sem("decay_exponents_ready")
        s_dexp = sem("decays_ready")
        s_kvT = sem("kv_transposed")
        s_kvc = sem("kv_copied")
        s_kk = sem("kk_qk_ready")
        s_A = sem("A_ready")
        s_AT = sem("A_transposed")
        s_ATc = sem("A_transposed_copied")
        s_X0 = sem("inverse_started")
        s_round = sem("doubling_products")
        s_P = sem("power_copied")
        s_X = sem("inverse_doubled")
        s_dec = sem("decayed_qk_ready")
        s_E = sem("off_diagonal_ready")
        s_w1 = sem("merge_first_product")
        s_w1c = sem("merge_first_copied")
        s_w2 = sem("merge_products")
        s_T = sem("merge_done")
        s_ks = sem("k_state_ready")
        s_rhs = sem("rhs_ready")
        s_vn = sem("v_new_ready")
        s_vnc = sem("v_new_copied")
        s_o = sem("gdn_out")
        s_oc2 = sem("gdn_out_copied")
        s_S = sem("state_ready")
        s_osq = sem("gdn_out_squared")
        s_oss = sem("gdn_out_summed")
        s_ort = sem("gdn_out_root")
        s_on = sem("gdn_out_normed")
        s_ot = sem("gdn_out_transposed")

        s_cdtab = sem("cd_tables_loaded")
        s_cdpad = sem("cd_pads_zeroed")
        s_cdc = sem("cd_chunk_copied")
        s_vT = sem("cd_v_transposed")
        s_vTc = sem("cd_v_copied")
        s_ws = sem("window_scores")
        s_wm = sem("window_max_ready")
        s_we = sem("window_exps_ready")
        s_wp = sem("window_probs_ready")
        s_wt = sem("window_probs_transposed")
        s_wtc = sem("window_probsT_copied")
        s_wo = sem("window_out")
        s_woc = sem("window_out_copied")
        s_z = sem("stick_scores")
        s_zc = sem("stick_scores_copied")
        s_sp = sem("stick_softplus_ready")
        s_lm = sem("stick_logs_ready")
        s_cum = sem("stick_cumulated")
        s_aw = sem("stick_exponents_ready")
        s_ae = sem("stick_exps_ready")
        s_am = sem("stick_weights_ready")
        s_so = sem("stick_out")
        s_soc = sem("stick_out_copied")

        block = ctx.enter_context(nc.Block())

        UNITS = 4

        def unit_shape(u):
            return ((8, P), (4, 2 * P), (4, 2 * P), (2, T))[u]

        def unit_scores(u):
            if u == 0:
                return [(4 * z, ps[:, z, :].rearrange("p (n c) -> p n c", c=P)) for z in range(2)]
            n, keys = unit_shape(u)
            return [(0, ps[:, 0:n, 0:keys])]

        def unit_probs(u):
            n, keys = unit_shape(u)
            return probs[:, u % 2, 0:n * keys].rearrange("p (n c) -> p n c", c=keys)

        GROUPS = ((0, 4), (4, 8), (8, 9))

        def blocks(bank, lo_, hi_):
            return ps[:, bank, 0:(hi_ - lo_) * P].rearrange("p (n c) -> p n c", c=P)

        def over(col, shape):
            return col.unsqueeze(2).to_broadcast(shape)

        def mask(n, count):
            return masks[:, n:n + 1, :].to_broadcast([P, count, P])

        subs, n, f = [], 0, 0
        for kind, layer in SUBLAYERS:
            subs.append((kind, n, layer, f))
            n += SIZES[kind]
            f += kind == "ffn"
        n_chunks = n

        def rows(n):
            for kind, b, _, _ in subs:
                if b <= n < b + SIZES[kind]:
                    return KH if kind == "ffn" and n - b >= 2 * NPAIR else KD

        def gain(layer, s, m):
            g = (layer * 6 + s) * KD + m
            return gains[:, g:g + 1]

        def norm_of(k):
            return 2 * (k % 3)

        def two(b):
            return ps[:, b:b + 2, 0:T]

        def pair_banks(j):
            return 4 - 4 * (j % 2)

        XB = 2

        @block.sync
        def _(sp):
            sp.dma_start(ident[:, :], c["c_ident"]).then_inc(s_const, 16)
            sp.dma_start(x_tok[:, 0, :], a["x"][0, 0:P, :]).then_inc(s_in, 16)
            sp.dma_start(x_tok[:, 1, :], a["x"][0, P:2 * P, :]).then_inc(s_in, 16)
            sp.dma_start(x_tok[0:N_META, 2, :], a["meta_tokens"]).then_inc(s_in, 16)
            sp.dma_start(cw_tok[:, :], a["ab_conv_w"][0].rearrange("k (m p) -> (k m) p", p=P)).then_inc(s_in, 16)
            sp.dma_start(g_tok[:, :], a["norm_gains"].rearrange("l s (m p) -> (l s m) p", p=P)).then_inc(s_in, 16)

            def load(n, src, i=0):
                sp.wait_ge(s_lo, n + 1 + i * NRAW)
                dst = raw[:, n % NRAW, 0:rows(n) * CB].rearrange("p (k c) -> p k c", c=CB)
                sp.dma_start(dst, src).then_inc(s_raw[n % NRAW], 16)

            for k, (kind, b, layer, f) in enumerate(subs):
                if kind == "ffn":
                    wg = a["ffn_w_gate"][layer, f % 2].rearrange("(k p) c -> p k c", p=P)
                    wu = a["ffn_w_up"][layer, f % 2].rearrange("(k p) c -> p k c", p=P)
                    wd = a["ffn_w_down"][layer, f % 2].rearrange("(k p) c -> p k c", p=P)
                    with sp.Fori(0, NPAIR // 2) as i:
                        for t in range(2):
                            load(b + 2 * t, wg[:, :, bass.ds(i * 2 * CB + t * CB, CB)], i)
                            load(b + 2 * t + 1, wu[:, :, bass.ds(i * 2 * CB + t * CB, CB)], i)
                    if k == 0:
                        for dst, src in ((masks[:, :, :], c["c_masks"]), (swap[:, :], c["c_swap"]),
                                         (head_of[:, :], c["c_head_of"]),
                                         (w_ba[:, :, :], a["ab_w_in"][0, :, AB_CHUNKS * CB:AB_IN].rearrange(
                                             "(k p) c -> p k c", p=P)),
                                         (dt4[:, :], a["ab_dt_bias"].to_broadcast([P, HG])),
                                         (alog4[:, :], a["ab_a_log"].to_broadcast([P, HG])),
                                         (out_norm[:, :], a["ab_out_norm"].rearrange("o p -> p o"))):
                            sp.dma_start(dst, src).then_inc(s_const, 16)
                    load(b + 2 * NPAIR - 2, wg[:, :, FF - CB:FF])
                    load(b + 2 * NPAIR - 1, wu[:, :, FF - CB:FF])
                    for blk in range(NBLK):
                        for half in range(2):
                            load(b + 2 * NPAIR + 2 * blk + half,
                                 wd[:, half * KH:(half + 1) * KH, blk * CB:(blk + 1) * CB])
                if kind == "ab":
                    w_in = a["ab_w_in"][0].rearrange("(k p) c -> p k c", p=P)
                    w_out = a["ab_w_out"][0].rearrange("(k p) c -> p k c", p=P)
                    for n, c0 in enumerate(AB_ORDER):
                        load(b + n, w_in[:, :, c0:c0 + CB])
                        if n == 4:
                            sp.wait_ge(s_used, NW + b + 1)
                            sp.dma_start(rope[:, :, :], c["c_rope"]).then_inc(s_tab, 16)
                            sp.dma_start(decay[:, :, :], c["c_decay"]).then_inc(s_tab, 16)
                    for blk in range(NBLK):
                        load(b + AB_CHUNKS + blk, w_out[:, :, blk * CB:(blk + 1) * CB])
                if kind == "cd":
                    w_in = a["cd_w_in"][0].rearrange("(k p) c -> p k c", p=P)
                    w_out = a["cd_w_out"][0].rearrange("(k p) c -> p k c", p=P)
                    for n in range(CD_CHUNKS):
                        load(b + n, w_in[:, :, n * CB:(n + 1) * CB])
                        if n == 4:
                            sp.wait_ge(s_used, NW + b + 1)
                            sp.dma_start(window[:, :, :], c["c_window"]).then_inc(s_cdtab, 16)
                            sp.dma_start(before[:, :], c["c_before"]).then_inc(s_cdtab, 16)
                            sp.dma_start(sinks8[:, 1, :], a["cd_sinks"].to_broadcast([P, HS])).then_inc(s_cdtab, 16)
                            for h in range(4):
                                sp.dma_start(sinks2[h * TAIL:(h + 1) * TAIL, :],
                                             a["cd_sinks"][:, 2 * h:2 * h + 2].to_broadcast([TAIL, 2])).then_inc(s_cdtab, 16)
                    for blk in range(NBLK):
                        load(b + CD_CHUNKS + blk, w_out[:, :, blk * CB:(blk + 1) * CB])
            for t in range(2):
                sp.wait_ge(s_oc, 2 * t + 2)
                sp.dma_start(out[0, t * P:(t + 1) * P, :], o_tok[:, t, :]).then_inc(s_out, 16)
            sp.wait_ge(s_out, 32)

        @block.gpsimd
        def _(pool):
            pool.memset(ones[:, :], 1.0).then_inc(s_ones, 1)
            for kind, b, _, _ in subs:
                if kind == "ab":
                    pool.wait_ge(s_used, NW + b + 1)
                    for t in (gq, gk, gv):
                        pool.memset(t[:, :, T:TP], 0.0).then_inc(s_pads, 1)
                    pool.memset(ba[:, :, :], 0.0).then_inc(s_pads, 1)
                if kind == "cd":
                    pool.wait_ge(s_used, NW + b + 1)
                    pool.memset(cq[:, :, T:TP], 0.0).then_inc(s_cdpad, 1)

        @block.scalar
        def _(act):
            step = Steps(act, s_act)

            def hi(n, i=0):
                if n >= n_chunks:
                    return
                act.wait_ge(s_raw[n % NRAW], 16 * (n // NRAW + 1) + i * 16)
                act.wait_ge(s_used, n + 1 + i * 4)
                act.activation(w_hi[:, n % NW, 0:rows(n) * CB], raw[:, n % NRAW, 0:rows(n) * CB], ACT.Copy)\
                    .then_inc(s_hi, 1)

            def silu(b, f, j, i=0):
                act.wait_ge(s_used, NW + b + 2 * j + 1 + i * 4)
                act.wait_ge(s_hid, NPAIR * f + j + 1 + i * 2)
                act.activation(gates[:, j % 2, :, :], two(pair_banks(j)), ACT.Silu).then_inc(s_silu, 1)

            def y_block(k, blk, n):
                q = NBLK * k + blk
                act.wait_ge(s_used, NW + n + 1)
                act.activation(yT[:, 2 * blk:2 * blk + 2, :], two(2 * blk), ACT.Copy)
                if q >= 2:
                    act.wait_ge(s_ss, q - 1)
                act.activation(y_sq[:, q % 2, :, :], two(2 * blk), ACT.Square).then_inc(s_ysq, 1)

            def inverse_root(slot, log_scale):
                step.done(act.activation(lnv[:, :], ps[:, slot, 0:T], ACT.Ln, bias=EPS, scale=1.0 / D))
                act.activation(rstd[:, slot, :], lnv[:, :], ACT.Exp, bias=log_scale, scale=-0.5).then_inc(s_rstd, 1)

            def post_norm(k, kind):
                act.wait_ge(s_ysum, k + 1)
                inverse_root(0, LN_HALF if kind == "ffn" else 0.0)

            def pre_norm(k):
                for g in range(KD // 2):
                    q = KD // 2 * k + g
                    act.wait_ge(s_h, q + 1)
                    if q >= 2:
                        act.wait_ge(s_hsum, q - 1)
                    act.activation(h_sq[:, q % 2, :, :], hT[:, 2 * g:2 * g + 2, :], ACT.Square).then_inc(s_hsq, 1)
                act.wait_ge(s_hsum, KD // 2 * (k + 1))
                inverse_root(1, 0.0)
                for m in range(KD):
                    act.wait_ge(s_u32, KD * k + m + 1)
                    act.activation(u_hi[:, m, :], yT[:, m, :], ACT.Copy).then_inc(s_uhi, 1)

            def split_hi(half):
                act.wait_ge(s_m32, half + 1)
                m = slice(4 * (half % 2), 4 * (half % 2) + 4)
                act.activation(u_hi[:, m, :], yT[:, m, :], ACT.Copy).then_inc(s_mhi, 1)

            def out_projection(k, b):
                for blk in range(NBLK):
                    hi(b + blk + 2) if blk < 3 else None
                    y_block(k, blk, b + blk)

            def ab(k, b):
                act.preload_act_table_set(SILU_SET)
                for st in range(AB_CHUNKS + 2):
                    if st <= AB_CHUNKS:
                        hi(b + st + 1)
                    n = st - 1
                    if n in AB_GATES:
                        act.wait_ge(s_used, NW + b + n + 1)
                        to, m = (rg, n - 6) if n < 8 else (gz, n - 8)
                        act.activation(to[:, 2 * m:2 * m + 2, :], two(2 * (n % 2)), ACT.Silu).then_inc(s_evac, 1)
                        if n == AB_GATES[-1]:
                            act.preload_act_table_set(EXP_SET)
                    if n in AB_ROT:
                        act.wait_ge(s_used, NW + b + n + 1)
                        if n > 10:
                            act.wait_ge(s_rot, n - 10)
                        act.activation(qraw[:, :, :], two(2 * (n % 2)), ACT.Copy).then_inc(s_evac, 1)
                    if n in AB_V:
                        act.wait_ge(s_used, NW + b + n + 1)
                        m = 2 * (n - 14)
                        act.activation(rv[:, m:m + 2, :], two(2 * (n % 2)), ACT.Copy).then_inc(s_evac, 1)
                    n = st - 2
                    if n in AB_CONV:
                        act.wait_ge(s_conv, n + 1)
                        to, m = (gq, gk, gv)[n // 2], 2 * (n % 2)
                        act.activation(to[:, m:m + 2, 0:T], cacc[:, n % 2, :, :], ACT.Silu).then_inc(s_csilu, 1)
                    v = st - 12
                    if 0 <= v < 4:
                        act.wait_ge(s_l2sum, v + 1)
                        if v:
                            act.wait_ge(s_l2, v)
                        step.done(act.activation(l2r[:, :, :], ps[:, 6:8, 0:TP], ACT.Ln, bias=EPS))
                        act.activation(l2r[:, :, :], l2r[:, :, :], ACT.Exp, scale=-0.5,
                                       bias=LN_QSCALE if v < 2 else 0.0).then_inc(s_l2r, 1)
                    v = st - 11
                    if 0 <= v < 4:
                        if v == 0:
                            act.wait_ge(s_pads, 4)
                            act.wait_ge(s_csilu, 4)
                        to, m = (gq, gk)[v // 2], 2 * (v % 2)
                        act.activation(l2sq[:, :, :], to[:, m:m + 2, :], ACT.Square).then_inc(s_l2sq, 1)
                for t, (_, n) in enumerate(TOK):
                    act.wait_ge(s_rvT, t + 1)
                    act.activation(rv_tok[0:n, t, :], ps[0:n, 4 + t, :], ACT.Copy).then_inc(s_rvc, 1)
                act.wait_ge(s_x, 1)
                step.done(act.activation(small[:, 2, :], small[:, 1, :], ACT.Exp, scale=-1.0))
                step.done(act.activation(small[:, 2, :], small[:, 2, :], ACT.Ln, bias=1.0))
                act.activation(small[:, 3, 0:HG], alog4[:, :], ACT.Exp)
                act.activation(small[:, 4, :].rearrange("p (t h) -> p t h", h=HG), ba[:, :, 0:HG], ACT.Exp, scale=-1.0)\
                    .then_inc(s_xe, 1)
                act.wait_ge(s_pv, 1)
                act.activation(ret[:, :, :], ps[:, 4:8, 0:T], ACT.Copy).then_inc(s_ret, 1)
                act.wait_ge(s_cent, 1)
                act.activation(attn[:, :, 0:T], ret[:, :, :], ACT.Square).then_inc(s_rsq, 1)
                act.wait_ge(s_var, 1)
                step.done(act.activation(attn[:, :, 0:T], ps[:, 4:8, 0:T], ACT.Ln, bias=EPS, scale=1.0 / P))
                act.activation(attn[:, :, 0:T], attn[:, :, 0:T], ACT.Exp, scale=-0.5).then_inc(s_rrt, 1)
                split_hi(0)
                act.wait_ge(s_dcl, 1)
                act.activation(dT[:, :, :], dT[:, :, :], ACT.Exp).then_inc(s_dexp, 1)
                act.activation(dN[:, :, :], dN[:, :, :], ACT.Exp, scale=-1.0).then_inc(s_dexp, 1)
                for lo_, hi_ in GROUPS:
                    act.activation(eG[:, lo_:hi_, :], blocks(4 + lo_ // 4, lo_, hi_), ACT.Exp).then_inc(s_dexp, 1)
                act.wait_ge(s_AT, 1)
                for lo_, hi_ in GROUPS:
                    act.activation(dmat[:, lo_:hi_, :], blocks(4 + lo_ // 4, lo_, hi_), ACT.Copy).then_inc(s_ATc, 1)
                for r in range(3):
                    for g, (lo_, hi_) in enumerate(GROUPS):
                        act.wait_ge(s_round, 3 * r + g + 1)
                        for z in range(2):
                            src = blocks(4 * g + z, lo_, hi_) if g < 2 else ps[:, 0, z * P:(z + 1) * P]
                            ins = act.activation(PP[:, z, lo_:hi_, :], src, ACT.Copy)
                        ins.then_inc(s_P, 1)
                for m in range(3):
                    for g, (lo_, hi_) in enumerate(GROUPS[:2]):
                        act.wait_ge(s_w1, 2 * m + g + 1)
                        act.activation(w1[:, lo_:hi_, :], blocks(4 * g, lo_, hi_), ACT.Copy).then_inc(s_w1c, 1)
                for t, (lo_, hi_) in enumerate(GROUPS):
                    act.wait_ge(s_vn, t + 1)
                    act.activation(vnew[:, 0:hi_ - lo_, :], blocks(1, lo_, hi_), ACT.Copy).then_inc(s_vnc, 1)
                    act.wait_ge(s_o, t + 1)
                    act.activation(O[:, lo_:hi_, :], blocks(2, lo_, hi_), ACT.Copy).then_inc(s_oc2, 1)
                act.wait_ge(s_oc2, 3)
                act.activation(PP[:, 0, :, :], O, ACT.Square).then_inc(s_osq, 1)
                act.wait_ge(s_oss, 1)
                step.done(act.activation(r9[:, :], r9[:, :], ACT.Ln, bias=EPS, scale=1.0 / P))
                act.activation(r9[:, :], r9[:, :], ACT.Exp, scale=-0.5).then_inc(s_ort, 1)
                split_hi(1)
                out_projection(k, b + AB_CHUNKS)

            def cd(k, b):
                for st in range(CD_CHUNKS + 1):
                    hi(b + st + 1)
                    n = st - 1
                    if n < 0:
                        continue
                    act.wait_ge(s_used, NW + b + n + 1)
                    bank = 2 * (n % 2)
                    if n < 2:
                        ins = act.activation(cq[:, 2 * n:2 * n + 2, 0:T], two(bank), ACT.Copy)
                    elif n == 2:
                        for head in range(2):
                            for half in range(2):
                                act.activation(kdup[half * DH:(half + 1) * DH, head, :],
                                               ps[head * DH:(head + 1) * DH, bank, 0:T], ACT.Copy)
                        ins = act.activation(cv[:, :], ps[:, bank + 1, 0:T], ACT.Copy)
                    else:
                        to, m = (sbq, sbk, sbv)[(n - 3) // 2], 2 * ((n - 3) % 2)
                        ins = act.activation(to[:, m:m + 2, :], two(bank), ACT.Copy)
                    ins.then_inc(s_cdc, 1)
                act.wait_ge(s_vT, 1)
                act.activation(cv_tok[:, 0:2, :], ps[:, 4, 0:2 * P].rearrange("p (t c) -> p t c", c=P), ACT.Copy)
                act.activation(cv_tok[0:16, 2, :], ps[0:16, 4, 2 * P:3 * P], ACT.Copy)
                for t in range(3):
                    act.activation(sbv_tok[:, t, :], ps[:, 5 + t, :], ACT.Copy).then_inc(s_vTc, 1)

                def stick_scores(x):
                    act.wait_ge(s_z, x + 1)
                    if x:
                        act.wait_ge(s_so, x)
                    act.activation(zs[:, :, :], ps[:, 0:4, 0:SBW], ACT.Copy, scale=DH ** -0.5).then_inc(s_zc, 1)
                    act.wait_ge(s_zc, x + 1)
                    step.done(act.activation(sp1[:, :, :], zs[:, :, :], ACT.Abs))
                    step.done(act.activation(sp1[:, :, :], sp1[:, :, :], ACT.Exp, scale=-1.0))
                    act.activation(sp1[:, :, :], sp1[:, :, :], ACT.Ln, bias=1.0).then_inc(s_sp, 1)

                def stick_exp(x):
                    act.wait_ge(s_aw, x + 1)
                    act.activation(zs[:, :, :], zs[:, :, :], ACT.Exp).then_inc(s_ae, 1)

                def stick_out(x):
                    act.wait_ge(s_so, x + 1)
                    act.activation(yT[:, 4 + 2 * x:6 + 2 * x, :], two(4), ACT.Copy).then_inc(s_soc, 1)

                for u in range(UNITS):
                    n, keys = unit_shape(u)
                    act.wait_ge(s_wm, u + 1)
                    for m in range(n):
                        act.activation(unit_probs(u)[:, m, :], unit_probs(u)[:, m, :], ACT.Exp,
                                       bias=wmx[:, u % 2, 0, m:m + 1], accum_out=wmx[:, u % 2, 2, m:m + 1])
                    act.activation(wmx[:, u % 2, 1, 0:n], wmx[:, u % 2, 3, 0:n], ACT.Exp).then_inc(s_we, 1)
                    act.wait_ge(s_wt, u + 1)
                    if u:
                        act.wait_ge(s_wo, u)
                    if u < 3:
                        for z in range(2):
                            ins = act.activation(probsT[:, 4 * z:4 * z + 4, :], blocks(4 + z, 0, 4), ACT.Copy)
                    else:
                        act.activation(probsT[:, 0:4, :], blocks(4, 0, 4), ACT.Copy)
                        ins = act.activation(probsT[0:16, 4:6, :], ps[0:16, 5, 0:2 * P].rearrange("p (n c) -> p n c", c=P),
                                             ACT.Copy)
                    ins.then_inc(s_wtc, 1)
                    act.wait_ge(s_wo, u + 1)
                    src = ps[:, 6 + u % 2, :]
                    if u == 0:
                        act.activation(yT[:, 0:4, 0:P], blocks(6, 0, 4), ACT.Copy).then_inc(s_woc, 1)
                    elif u < 3:
                        act.activation(yT[:, 2 * u - 2:2 * u, P:2 * P], blocks(6 + u % 2, 0, 2), ACT.Copy).then_inc(s_woc, 1)
                    else:
                        act.activation(yT[:, 0:4, 2 * P:T], src[:, 0:64].rearrange("p (n c) -> p n c", c=16), ACT.Copy)\
                            .then_inc(s_woc, 1)
                act.wait_ge(s_woc, UNITS)
                act.activation(u_hi[:, 0:4, :], yT[:, 0:4, :], ACT.Copy).then_inc(s_mhi, 1)
                for x in range(2):
                    stick_scores(x)
                    stick_exp(x)
                    stick_out(x)
                act.wait_ge(s_soc, 2)
                act.activation(u_hi[:, 4:8, :], yT[:, 4:8, :], ACT.Copy).then_inc(s_mhi, 1)
                out_projection(k, b + CD_CHUNKS)

            act.preload_act_table_set(EXP_SET)
            hi(0)
            for k, (kind, b, layer, f) in enumerate(subs):
                pre_norm(k)
                if kind == "ffn":
                    act.preload_act_table_set(SILU_SET)
                    hi(b + 1)
                    hi(b + 2)
                    with act.Fori(0, (NPAIR - 3) // 2) as i:
                        for s in (1, 2):
                            hi(b + 2 * s + 1, i)
                            silu(b, f, s - 1, i)
                            hi(b + 2 * s + 2, i)
                    for s in range(NPAIR - 2, NPAIR + NBLK):
                        hi(b + 2 * s + 1)
                        if s <= NPAIR:
                            silu(b, f, s - 1)
                            if s == NPAIR:
                                act.preload_act_table_set(EXP_SET)
                        else:
                            blk = s - NPAIR - 1
                            y_block(k, blk, b + 2 * s - 1)
                        hi(b + 2 * s + 2)
                    y_block(k, NBLK - 1, b + SIZES[kind] - 1)
                elif kind == "ab":
                    ab(k, b)
                else:
                    cd(k, b)
                post_norm(k, kind)

        @block.vector
        def _(dve):
            step = Steps(dve, s_dve)
            dve.sem_inc(s_lo, NRAW)
            dve.sem_inc(s_hid, 2)

            def lo(n, i=0):
                if n >= n_chunks:
                    return
                dve.wait_ge(s_hi, n + 1 + i * 4)
                src, dst = raw[:, n % NRAW, 0:rows(n) * CB], w_lo[:, n % NW, 0:rows(n) * CB]
                dve.tensor_tensor(dst, src, w_hi[:, n % NW, 0:rows(n) * CB].bitcast(F32), ALU.subtract)\
                    .then_inc(s_lo, 1)

            def hidden(b, f, j, i=0):
                dve.wait_ge(s_used, NW + b + 2 * j + 2 + i * 4)
                dve.wait_ge(s_silu, NPAIR * f + j + 1 + i * 2)
                dve.wait_ge(s_hid, NPAIR * f + j + 1 + i * 2)
                step.done(dve.tensor_tensor(prod[:, j % 2, :, :], gates[:, j % 2, :, :], two(pair_banks(j) + 2), ALU.mult))
                to = bass.ds(i * 4 + 2 * j, 2)
                step.done(dve.tensor_copy(hid_hi[:, to, :], prod[:, j % 2, :, :]))
                dve.tensor_tensor(hid_lo[:, to, :], prod[:, j % 2, :, :], hid_hi[:, to, :].bitcast(F32), ALU.subtract)\
                    .then_inc(s_hid, 1)

            def add_squares(k, blk):
                q = NBLK * k + blk
                dve.wait_ge(s_ysq, q + 1)
                if blk == 0:
                    if k:
                        dve.wait_ge(s_ysum, k)
                    dve.tensor_tensor(ss[:, :], y_sq[:, q % 2, 0, :], y_sq[:, q % 2, 1, :], ALU.add).then_inc(s_ss, 1)
                else:
                    dve.wait_ge(s_ss, q)
                    step.done(dve.tensor_tensor(ss[:, :], ss[:, :], y_sq[:, q % 2, 0, :], ALU.add))
                    dve.tensor_tensor(ss[:, :], ss[:, :], y_sq[:, q % 2, 1, :], ALU.add).then_inc(s_ss, 1)

            def normed_input(k, layer):
                dve.wait_ge(s_rstd, 2 * k + 1)
                for m in range(KD + 1):
                    if m < KD:
                        dve.scalar_tensor_tensor(yT[:, m, :], hT[:, m, :], gain(layer, norm_of(k), m), rstd[:, 1, :],
                                                 ALU.mult, ALU.mult).then_inc(s_u32, 1)
                    if m:
                        dve.wait_ge(s_uhi, KD * k + m)
                        dve.tensor_tensor(u_lo[:, m - 1, :], yT[:, m - 1, :], u_hi[:, m - 1, :].bitcast(F32),
                                          ALU.subtract).then_inc(s_ulo, 1)

            def update_h(k, layer):
                dve.wait_ge(s_rstd, 2 * k + 2)
                for g in range(KD // 2):
                    for m in (2 * g, 2 * g + 1):
                        ins = dve.scalar_tensor_tensor(yT[:, m, :], yT[:, m, :], gain(layer, norm_of(k) + 1, m),
                                                       rstd[:, 0, :], ALU.mult, ALU.mult)
                        if m % 2:
                            step.done(ins)
                    dve.tensor_tensor(hT[:, 2 * g:2 * g + 2, :], hT[:, 2 * g:2 * g + 2, :], yT[:, 2 * g:2 * g + 2, :],
                                      ALU.add).then_inc(s_h, 1)

            def split_lo(half):
                dve.wait_ge(s_mhi, half + 1)
                m = slice(4 * (half % 2), 4 * (half % 2) + 4)
                dve.tensor_tensor(u_lo[:, m, :], yT[:, m, :], u_hi[:, m, :].bitcast(F32), ALU.subtract).then_inc(s_mlo, 1)

            def out_projection(k, b):
                for blk in range(NBLK):
                    lo(b + blk + 2) if blk < 3 else None
                    add_squares(k, blk)

            def conv(n):
                for m in range(2):
                    src, tile_ = ps[:, 2 * (n % 2) + m, :], 2 * n + m
                    acc = cacc[:, n % 2, m, :]
                    step.done(dve.tensor_scalar(acc, src[:, 0:T], convw[:, 36 + tile_:37 + tile_], None, ALU.mult))
                    for d in range(1, 4):
                        w = convw[:, (3 - d) * 12 + tile_:(3 - d) * 12 + tile_ + 1]
                        ins = dve.scalar_tensor_tensor(acc[:, d:T], src[:, 0:T - d], w, acc[:, d:T], ALU.mult, ALU.add)
                        if d < 3:
                            step.done(ins)
                        elif m == 0:
                            step.done(ins)
                        else:
                            ins.then_inc(s_conv, 1)

            def ab(k, b):
                for st in range(AB_CHUNKS + 2):
                    if st <= AB_CHUNKS:
                        lo(b + st + 1)
                    n = st - 1
                    if n in AB_CONV:
                        dve.wait_ge(s_used, NW + b + n + 1)
                        if n >= 2:
                            dve.wait_ge(s_csilu, n - 1)
                        conv(n)
                    if n == 0:
                        dve.wait_ge(s_ba, 1)
                        dve.wait_ge(s_pads, 4)
                        dve.tensor_copy(ba[:, 0:2, :], ps[:, 7, 0:16].rearrange("p (t c) -> p t c", c=2 * HG))
                        for h in range(HG):
                            ins = dve.tensor_copy(ba[h * TAIL:h * TAIL + 16, 2, :], ps[h * TAIL:h * TAIL + 16, 7, 16:24])
                        ins.then_inc(s_bac, 1)
                    n = st - 2
                    if n in AB_ROT:
                        dve.wait_ge(s_swap, n - 10 + 1)
                        if n == 10:
                            dve.wait_ge(s_tab, 32)
                        to, m = (rq, rk)[(n - 10) // 2], 2 * (n % 2)
                        cos, sin = (rope[:, z:z + 1, :].to_broadcast([P, 2, T]) for z in range(2))
                        step.done(dve.tensor_tensor(rot[:, :, :], two(4), sin, ALU.mult))
                        step.done(dve.tensor_tensor(to[:, m:m + 2, :], qraw[:, :, :], cos, ALU.mult))
                        dve.tensor_tensor(to[:, m:m + 2, :], to[:, m:m + 2, :], rot[:, :, :], ALU.add).then_inc(s_rot, 1)
                        dve.wait_ge(s_rot, n - 10 + 1)
                    v = st - 12
                    if 0 <= v < 4:
                        dve.wait_ge(s_l2r, v + 1)
                        to, m = (gq, gk)[v // 2], 2 * (v % 2)
                        dve.tensor_tensor(to[:, m:m + 2, :], to[:, m:m + 2, :], l2r[:, :, :], ALU.mult).then_inc(s_l2, 1)
                sm = [small[:, n, :].rearrange("p (t h) -> p t h", h=HG) for n in range(8)]
                dve.wait_ge(s_bac, 1)
                dve.wait_ge(s_const, 16 * 8)
                step.done(dve.tensor_tensor(sm[0], ba[:, :, HG:2 * HG],
                                            dt4[:, :].unsqueeze(1).to_broadcast([P, 3, HG]), ALU.add))
                dve.scalar_tensor_tensor(small[:, 1, :], small[:, 0, :], -1.0, small[:, 0, :], ALU.mult, ALU.max)\
                    .then_inc(s_x, 1)
                dve.wait_ge(s_score, 1)
                dve.tensor_tensor(attn[:, :, 0:T], ps[:, 0:4, 0:T], decay[:, :, :], ALU.mult)
                dve.tensor_tensor(attn[:, :, T:2 * T - P], ps[:, 0:4, T:2 * T - P], decay[:, :, 0:T - P], ALU.mult)
                dve.tensor_tensor(attn[0:16, :, 2 * T - P:2 * T - P + 16], ps[0:16, 0:4, 2 * T - P:2 * T - P + 16],
                                  decay[0:16, :, 0:16], ALU.mult).then_inc(s_attn, 1)
                dve.wait_ge(s_xe, 1)
                step.done(dve.scalar_tensor_tensor(small[:, 5, :], small[:, 0, :], 0.0, small[:, 2, :], ALU.max, ALU.add))
                step.done(dve.scalar_tensor_tensor(sm[6], sm[5], -1.0,
                                                   small[:, 3, 0:HG].unsqueeze(1).to_broadcast([P, 3, HG]),
                                                   ALU.mult, ALU.mult))
                step.done(dve.tensor_scalar(small[:, 4, :], small[:, 4, :], 1.0, None, ALU.add))
                step.done(dve.reciprocal(small[:, 7, :], small[:, 4, :]))
                for to, n in ((g9, 6), (beta9, 7)):
                    dve.tensor_copy(to[:, 0:8], small[:, n, 0:8])
                    step.done(dve.tensor_tensor(small[:, n, 8:12], small[:, n, 8:12], head_of[:, :], ALU.mult))
                    ins = dve.tensor_reduce(to[:, 8:9], small[:, n, 8:12], AX.X, ALU.add)
                    if to is g9:
                        step.done(ins)
                ins.then_inc(s_g9, 1)
                dve.wait_ge(s_mean, 1)
                dve.scalar_tensor_tensor(ret[:, :, :], ps[:, 0:4, 0:T], -1.0 / P, ret[:, :, :], ALU.mult, ALU.add)\
                    .then_inc(s_cent, 1)
                dve.wait_ge(s_cent, 1)
                step.done(dve.tensor_tensor(rg[:, :, :], rg[:, :, :], ret[:, :, :], ALU.mult))
                dve.wait_ge(s_rrt, 1)
                dve.tensor_tensor(yT[:, 0:4, :], rg[:, :, :], attn[:, :, 0:T], ALU.mult).then_inc(s_m32, 1)
                split_lo(0)
                dve.wait_ge(s_gsum, 1)
                step.done(dve.tensor_copy(gc9[:, :], ps[:, 7, 0:9]))
                for lo_, hi_ in GROUPS:
                    ins = dve.tensor_tensor(dmat[:, lo_:hi_, :], blocks(4 + lo_ // 4, lo_, hi_),
                                            over(gc9[:, lo_:hi_], [P, hi_ - lo_, P]), ALU.subtract)
                step.done(ins)
                dve.tensor_scalar(dT[:, :, :], dmat[:, :, :], 0.0, None, ALU.min)
                dve.tensor_scalar(dN[:, :, :], dmat[:, :, :], 0.0, None, ALU.max).then_inc(s_dcl, 1)
                dve.wait_ge(s_dexp, 1)
                dve.tensor_tensor(dT[:, 0:8, :], dT[:, 0:8, :], mask(UPPER, 8), ALU.mult)
                step.done(dve.tensor_tensor(dT[:, 8, :], dT[:, 8, :], masks[:, UPPER32, :], ALU.mult))
                dve.wait_ge(s_kvT, 1)
                for g, (lo_, hi_) in enumerate(GROUPS[:2]):
                    dve.tensor_tensor(ktail[:, lo_:hi_, :], blocks(g, lo_, hi_),
                                      dT[:, lo_:hi_, P - 1:P].to_broadcast([P, 4, P]), ALU.mult)
                for g, (lo_, hi_) in enumerate(GROUPS):
                    src = blocks(2 + g, lo_, hi_) if g < 2 else ps[:, 7, P:2 * P].unsqueeze(1)
                    ins = dve.tensor_tensor(R[:, lo_:hi_, :], src, over(beta9[:, lo_:hi_], [P, hi_ - lo_, P]), ALU.mult)
                ins.then_inc(s_kvc, 1)
                dve.wait_ge(s_dexp, 2)
                dve.tensor_tensor(dN[:, 0:8, :], dN[:, 0:8, :], mask(LOWER, 8), ALU.mult)
                step.done(dve.tensor_tensor(dN[:, 8, :], dN[:, 8, :], masks[:, LOWER32, :], ALU.mult))
                step.done(dve.tensor_tensor(dN[:, :, :], dN[:, :, :], over(beta9[:, :], [P, 9, P]), ALU.mult))
                dve.wait_ge(s_kk, 2)
                for g, (lo_, hi_) in enumerate(GROUPS):
                    src = blocks(g, lo_, hi_) if g < 2 else ps[:, 7, 2 * P:3 * P].unsqueeze(1)
                    ins = dve.tensor_tensor(dN[:, lo_:hi_, :], dN[:, lo_:hi_, :], src, ALU.mult)
                ins.then_inc(s_A, 1)
                for g, (lo_, hi_) in enumerate(GROUPS):
                    src = blocks(2 + g, lo_, hi_) if g < 2 else ps[:, 7, 3 * P:4 * P].unsqueeze(1)
                    ins = dve.tensor_tensor(dT[:, lo_:hi_, :], dT[:, lo_:hi_, :], src, ALU.mult)
                step.done(ins)
                dve.wait_ge(s_A, 1)
                for g, (lo_, hi_) in enumerate(GROUPS):
                    n = hi_ - lo_
                    dve.tensor_tensor(PP[:, 0, lo_:hi_, :], dN[:, lo_:hi_, :], mask(DIAG16, n), ALU.mult)
                    dve.wait_ge(s_ATc, g + 1)
                    step.done(dve.tensor_tensor(PP[:, 1, lo_:hi_, :], dmat[:, lo_:hi_, :], mask(DIAG16, n), ALU.mult))
                    for z in range(2):
                        ins = dve.tensor_tensor(XX[:, z, lo_:hi_, :], PP[:, z, lo_:hi_, :],
                                                ident[:, :].unsqueeze(1).to_broadcast([P, n, P]), ALU.add)
                    ins.then_inc(s_X0, 1)
                dve.wait_ge(s_dexp, 5)
                for t in (gq, gk):
                    dve.tensor_tensor(t[:, :, P:2 * P], t[:, :, P:2 * P], eG[:, 4:8, :], ALU.mult)
                    dve.tensor_tensor(t[:, :, 2 * P:TP], t[:, :, 2 * P:TP],
                                      eG[:, 8, :].rearrange("p (h t) -> p h t", t=TAIL), ALU.mult)
                egl = small[:, 0, 0:HG]
                step.done(dve.tensor_copy(egl.unsqueeze(2), eG[:, 4:8, P - 1:P]))
                for r in range(1, 4):
                    for g, (lo_, hi_) in enumerate(GROUPS):
                        dve.wait_ge(s_round, 3 * r + g + 1)
                        for z in range(2):
                            src = blocks(4 * g + 2 + z, lo_, hi_) if g < 2 else ps[:, 2, z * P:(z + 1) * P].unsqueeze(1)
                            ins = dve.tensor_tensor(XX[:, z, lo_:hi_, :], XX[:, z, lo_:hi_, :], src, ALU.add)
                        ins.then_inc(s_X, 1)
                for m in range(3):
                    for g, (lo_, hi_) in enumerate(GROUPS[:2]):
                        dve.wait_ge(s_ATc, 3)
                        if m:
                            dve.wait_ge(s_w1, 2 * (m - 1) + g + 1)
                        dve.tensor_tensor(off_diag[:, lo_:hi_, :], dmat[:, lo_:hi_, :], mask(MERGE + m, 4), ALU.mult)\
                            .then_inc(s_E, 1)
                    for g, (lo_, hi_) in enumerate(GROUPS[:2]):
                        dve.wait_ge(s_w2, 2 * m + g + 1)
                        if m == 0:
                            dve.wait_ge(s_X, 9)
                        for z in ((0, 1) if m < 2 else (1,)):
                            ins = dve.tensor_tensor(XX[:, z, lo_:hi_, :], XX[:, z, lo_:hi_, :],
                                                    blocks(4 * g + 2 + z, lo_, hi_), ALU.subtract)
                        ins.then_inc(s_T, 1)
                for t, (lo_, hi_) in enumerate(GROUPS):
                    n = hi_ - lo_
                    if t:
                        dve.wait_ge(s_ks, t)
                        step.done(dve.tensor_tensor(vtmp[:, 0:n, :], blocks(0, lo_, hi_),
                                                    over(beta9[:, lo_:hi_], [P, n, P]), ALU.mult))
                        dve.tensor_tensor(R[:, lo_:hi_, :], R[:, lo_:hi_, :], vtmp[:, 0:n, :], ALU.subtract)\
                            .then_inc(s_rhs, 1)
                    if t == 0:
                        dve.wait_ge(s_o, 1)
                        dve.tensor_copy(S[:, :, :], blocks(3, 0, 4)).then_inc(s_S, 1)
                    if t == 1:
                        dve.wait_ge(s_o, 2)
                        step.done(dve.tensor_tensor(S[:, :, :], S[:, :, :], over(egl, [P, HG, P]), ALU.mult))
                        dve.tensor_tensor(S[:, :, :], S[:, :, :], blocks(3, 0, 4), ALU.add).then_inc(s_S, 1)
                dve.wait_ge(s_osq, 1)
                dve.tensor_reduce(r9[:, :], PP[:, 0, :, :], AX.X, ALU.add).then_inc(s_oss, 1)
                dve.wait_ge(s_ort, 1)
                dve.tensor_tensor(O, O, over(r9[:, :], [P, 9, P]), ALU.mult).then_inc(s_on, 1)
                dve.wait_ge(s_ot, 1)
                for t, (c0, n) in enumerate(TOK):
                    src = blocks(4 + t, 0, 4) if t < 2 else \
                        ps[:, 6, 0:P].rearrange("p (h t) -> p h t", t=TAIL)[:, :, 0:n]
                    ins = dve.scalar_tensor_tensor(yT[:, 4:8, c0:c0 + n], src, out_norm[:, :], gz[:, :, c0:c0 + n],
                                                   ALU.mult, ALU.mult)
                ins.then_inc(s_m32, 1)
                split_lo(1)
                out_projection(k, b + AB_CHUNKS)

            def cd(k, b):
                for st in range(CD_CHUNKS + 1):
                    lo(b + st + 1)
                dve.wait_ge(s_cdtab, 16 * 7)
                step.done(dve.tensor_copy(sinks8[:, 0, :].rearrange("p (s a) -> p s a", s=2),
                                          sinks8[:, 1, :].rearrange("p (a s) -> p s a", s=2)))
                for u in range(UNITS):
                    n, keys = unit_shape(u)
                    t = (0, 1, 1, 2)[u]
                    sink = (sinks8[:, 0, :], sinks8[:, 1, 0:4], sinks8[:, 1, 4:8], sinks2[:, :])[u]
                    neg_max, sink_exp, total, sink_arg = (wmx[:, u % 2, z, 0:n] for z in range(4))
                    dve.wait_ge(s_ws, u + 1)
                    if u >= 2:
                        dve.wait_ge(s_wt, u - 1)
                    for m0, src in unit_scores(u):
                        w = src.shape[1]
                        ins = dve.scalar_tensor_tensor(unit_probs(u)[:, m0:m0 + w, :], src, DH ** -0.5,
                                                       window[:, t:t + 1, 0:keys].to_broadcast([P, w, keys]),
                                                       ALU.mult, ALU.add)
                    step.done(ins)
                    step.done(dve.tensor_reduce(neg_max, unit_probs(u), AX.X, ALU.max))
                    step.done(dve.tensor_tensor(neg_max, neg_max, sink, ALU.max))
                    step.done(dve.tensor_tensor(sink_arg, sink, neg_max, ALU.subtract))
                    dve.tensor_scalar(neg_max, neg_max, -1.0, None, ALU.mult).then_inc(s_wm, 1)
                    dve.wait_ge(s_we, u + 1)
                    step.done(dve.tensor_tensor(total, total, sink_exp, ALU.add))
                    step.done(dve.reciprocal(total, total))
                    dve.tensor_tensor(unit_probs(u), unit_probs(u), over(total, [P, n, keys]), ALU.mult).then_inc(s_wp, 1)
                split_lo(2)
                for x in range(2):
                    dve.wait_ge(s_zc, x + 1)
                    step.done(dve.tensor_scalar(lb[:, :, :], zs[:, :, :], 0.0, None, ALU.min))
                    dve.wait_ge(s_sp, x + 1)
                    step.done(dve.tensor_tensor(lb[:, :, :], lb[:, :, :], sp1[:, :, :], ALU.subtract))
                    step.done(dve.tensor_tensor(lm[:, :, :], lb[:, :, :], zs[:, :, :], ALU.subtract))
                    valid = before[:, :].unsqueeze(1).to_broadcast([P, 4, SBW])
                    dve.tensor_tensor(lm[:, :, :], lm[:, :, :], valid, ALU.mult).then_inc(s_lm, 1)
                    dve.wait_ge(s_cum, x + 1)
                    dve.tensor_tensor(zs[:, :, :], lb[:, :, :], ps[:, 4:8, 0:SBW], ALU.add).then_inc(s_aw, 1)
                    dve.wait_ge(s_ae, x + 1)
                    dve.tensor_tensor(zs[:, :, :], zs[:, :, :], valid, ALU.mult).then_inc(s_am, 1)
                split_lo(3)
                out_projection(k, b + CD_CHUNKS)

            for g in range(2):
                dve.wait_ge(s_xT, 3 * g + 3)
                for t, (n, c0) in enumerate(((P, N_META), (P, N_META + P), (N_META, 0))):
                    src = ps[:, XB + 2 * t + g, 0:4 * n].rearrange("p (m t) -> p m t", m=4)
                    ins = dve.tensor_copy(hT[:, 4 * g:4 * g + 4, c0:c0 + n], src)
                ins.then_inc(s_h, 2)
            dve.wait_ge(s_gT, 1)
            step.done(dve.tensor_copy(gains[:, :], ps[:, 0, 0:12 * KD]))
            dve.wait_ge(s_cwT, 1)
            dve.tensor_copy(convw[:, :], ps[:, 1, 0:4 * 12]).then_inc(s_cwc, 1)
            lo(0)
            for k, (kind, b, layer, f) in enumerate(subs):
                normed_input(k, layer)
                if kind == "ffn":
                    lo(b + 1)
                    lo(b + 2)
                    with dve.Fori(0, (NPAIR - 3) // 2) as i:
                        step.enter(i, 4)
                        for s in (1, 2):
                            lo(b + 2 * s + 1, i)
                            hidden(b, f, s - 1, i)
                            lo(b + 2 * s + 2, i)
                    step.leave(4, (NPAIR - 3) // 2)
                    for s in range(NPAIR - 2, NPAIR + NBLK):
                        lo(b + 2 * s + 1)
                        if s <= NPAIR:
                            hidden(b, f, s - 1)
                        else:
                            add_squares(k, s - NPAIR - 1)
                        lo(b + 2 * s + 2)
                    add_squares(k, NBLK - 1)
                elif kind == "ab":
                    ab(k, b)
                else:
                    cd(k, b)
                update_h(k, layer)
            for t in range(2):
                for g in range(2):
                    dve.wait_ge(s_oT, 2 * t + g + 1)
                    dve.tensor_copy(o_tok[:, t, g * BANK:(g + 1) * BANK], ps[:, 2 + 2 * t + g, :]).then_inc(s_oc, 1)

        @block.tensor
        def _(pe):
            pe.sem_inc(s_used, NW)

            def tiles(n, bank, rhs_hi, rhs_lo, i=0, first=True, last=True, ready=None):
                pe.wait_ge(s_lo, NRAW + n + 1 + i * 4)
                for m in range(2):
                    for kk in range(rows(n)):
                        if ready and m == 0:
                            ready(kk)
                        w = slice(kk * CB + m * P, kk * CB + m * P + P)
                        wh, wl = w_hi[:, n % NW, w], w_lo[:, n % NW, w]
                        o = ps[:, bank + m, 0:T]
                        pe.matmul(o, wh, rhs_hi[:, kk, :], start=first and kk == 0, stop=False)
                        pe.matmul(o, wh, rhs_lo[:, kk, :], start=False, stop=False)
                        ins = pe.matmul(o, wl, rhs_hi[:, kk, :], start=False, stop=last and kk == rows(n) - 1)
                ins.then_inc(s_used, 1)

            def pair(b, f, j, i=0, ready=None):
                pe.wait_ge(s_hid, NPAIR * f + j + 1 + i * 2)
                tiles(b + 2 * j, pair_banks(j), u_hi, u_lo, i, ready=ready)
                tiles(b + 2 * j + 1, pair_banks(j) + 2, u_hi, u_lo, i)

            def pre_norm_sum(k):
                for g in range(KD // 2):
                    q = KD // 2 * k + g
                    pe.wait_ge(s_hsq, q + 1)
                    for m in range(2):
                        ins = pe.matmul(ps[:, 1, 0:T], ones[:, :], h_sq[:, q % 2, m, :],
                                        start=g == 0 and m == 0, stop=g == KD // 2 - 1 and m == 1)
                    ins.then_inc(s_hsum, 1)

            def post_norm_sum(k):
                pe.wait_ge(s_ss, NBLK * (k + 1))
                pe.matmul(ps[:, 0, 0:T], ones[:, :], ss[:, :], start=True, stop=True).then_inc(s_ysum, 1)

            def out_projection(b, half0):
                for blk in range(NBLK):
                    def ready(kk):
                        if kk % 4 == 0:
                            pe.wait_ge(s_mlo, half0 + kk // 4 + 1)
                    tiles(b + blk, 2 * blk, u_hi, u_lo, ready=ready if blk == 0 else None)

            def mm(o, lhsT, rhs, start=True, stop=True):
                return pe.matmul(o, lhsT, rhs, start=start, stop=stop, skip_group_check=True)

            def ab(k, b, ready):
                for n in range(AB_CHUNKS):
                    if n >= 2:
                        if n - 2 in AB_CONV:
                            pe.wait_ge(s_conv, n - 1)
                        else:
                            pe.wait_ge(s_evac, n - 7)
                    tiles(b + n, 2 * (n % 2), u_hi, u_lo, ready=ready if n == 0 else None)
                    if n == 0:
                        pe.wait_ge(s_const, 16 * 8)
                        for t, (c0, w) in enumerate(TOK):
                            for h in range(HG if t == 2 else 1):
                                o = ps[h * TAIL:h * TAIL + w, 7, 8 * t:8 * t + 8]
                                for kk in range(KD):
                                    ins = mm(o, yT[:, kk, c0:c0 + w], w_ba[:, kk, :], kk == 0, kk == KD - 1)
                        ins.then_inc(s_ba, 1)
                    if n - 1 in AB_ROT:
                        pe.wait_ge(s_evac, n - 6)
                        if n > 11:
                            pe.wait_ge(s_rot, n - 11)
                        for m in range(2):
                            ins = mm(ps[:, 4 + m, 0:T], swap[:, :], qraw[:, m, :])
                        ins.then_inc(s_swap, 1)
                    v = n - 11
                    if 0 <= v < 4:
                        pe.wait_ge(s_l2sq, v + 1)
                        pe.wait_ge(s_bac, 1)
                        if v:
                            pe.wait_ge(s_l2r, v)
                        for m in range(2):
                            ins = mm(ps[:, 6 + m, 0:TP], ones[:, :], l2sq[:, m, :])
                        ins.then_inc(s_l2sum, 1)
                pe.wait_ge(s_rot, 4)
                pe.wait_ge(s_l2r, 4)
                pe.wait_ge(s_evac, 10)
                for t, (c0, n) in enumerate(TOK):
                    for h in range(HR):
                        ins = pe.transpose(ps[0:n, 4 + t, h * P:(h + 1) * P], rv[:, h, c0:c0 + n], ident[:, :])
                    ins.then_inc(s_rvT, 1)
                off = 0
                for t, (c0, n) in enumerate(TOK):
                    for h in range(HR):
                        ins = mm(ps[0:n, h, off:off + T - c0], rk[:, h, c0:c0 + n], rq[:, h, c0:T])
                    off += T - c0
                ins.then_inc(s_score, 1)
                pe.wait_ge(s_attn, 1)
                pe.wait_ge(s_rvc, 3)
                for h in range(HR):
                    off = 0
                    for t, (c0, n) in enumerate(TOK):
                        ins = mm(ps[:, 4 + h, c0:T], rv_tok[0:n, t, h * P:(h + 1) * P], attn[0:n, h, off:off + T - c0],
                                 t == 0, t == 2)
                        off += T - c0
                ins.then_inc(s_pv, 1)
                pe.wait_ge(s_ret, 1)
                for h in range(HR):
                    ins = mm(ps[:, h, 0:T], ones[:, :], ret[:, h, :])
                ins.then_inc(s_mean, 1)
                pe.wait_ge(s_rsq, 1)
                for h in range(HR):
                    ins = mm(ps[:, 4 + h, 0:T], ones[:, :], attn[:, h, 0:T])
                ins.then_inc(s_var, 1)
                pe.wait_ge(s_rrt, 1)
                pe.wait_ge(s_g9, 1)
                mm(ps[:, 7, 0:8], masks[:, UPPER, :], g9[:, 0:8])
                mm(ps[:, 7, 8:9], masks[:, UPPER32, :], g9[:, 8:9])
                for q in range(9):
                    ins = mm(ps[:, 4 + q // 4, q % 4 * P:(q % 4 + 1) * P], g9[:, q:q + 1].to_broadcast([P, P]),
                             masks[:, UPPER if q < 8 else UPPER32, :])
                ins.then_inc(s_gsum, 1)

                def feat(x, q):
                    return x[:, q % 4, q // 4 * P:(q // 4 + 1) * P]

                def tails(bank, c0, x, rhs):
                    for h in range(HG):
                        ins = mm(ps[h * TAIL:(h + 1) * TAIL, bank, c0:c0 + P], x[:, h, 2 * P:TP], rhs(h))
                    return ins

                pe.wait_ge(s_l2, 4)
                pe.wait_ge(s_csilu, 6)
                pe.wait_ge(s_cent, 1)
                pe.wait_ge(s_dcl, 1)
                for q in range(8):
                    pe.transpose(ps[:, q // 4, q % 4 * P:(q % 4 + 1) * P], feat(gk, q), ident[:, :])
                for q in range(8):
                    pe.transpose(ps[:, 2 + q // 4, q % 4 * P:(q % 4 + 1) * P], feat(gv, q), ident[:, :])
                tails(7, P, gv, lambda h: ident[:, :]).then_inc(s_kvT, 1)
                pe.wait_ge(s_kvc, 1)
                for z, x in enumerate((gk, gq)):
                    for q in range(8):
                        mm(ps[:, 2 * z + q // 4, q % 4 * P:(q % 4 + 1) * P], feat(gk, q), feat(x, q))
                    tails(7, (2 + z) * P, gk, lambda h: x[:, :, 2 * P:TP]).then_inc(s_kk, 1)
                pe.wait_ge(s_A, 1)
                pe.wait_ge(s_dexp, 5)
                for q in range(9):
                    ins = pe.transpose(ps[:, 4 + q // 4, q % 4 * P:(q % 4 + 1) * P], dN[:, q, :], ident[:, :])
                ins.then_inc(s_AT, 1)
                for r in range(4):
                    for g, (lo_, hi_) in enumerate(GROUPS):
                        if r == 0:
                            pe.wait_ge(s_X0, g + 1)
                            if g == 1:
                                pe.wait_ge(s_X0, 3)
                                pe.wait_ge(s_ATc, 3)
                        copied = (3 * r, 3 * r - 1, min(3 * r + 1, 9))[g]
                        added = (3 * r - 3, 3 * r - 4, 3 * r - 2)[g]
                        if r or g == 2:
                            pe.wait_ge(s_P, copied)
                        if added > 0:
                            pe.wait_ge(s_X, added)
                        for q in range(lo_, hi_):
                            def o(z):
                                return ps[:, 4 * g + z, (q - lo_) * P:(q - lo_ + 1) * P] if g < 2 else \
                                    ps[:, z - z % 2, z % 2 * P:(z % 2 + 1) * P]
                            p_, pt, x_, xt = PP[:, 0, q, :], PP[:, 1, q, :], XX[:, 0, q, :], XX[:, 1, q, :]
                            if r < 3:
                                mm(o(0), pt, p_)
                                ins = mm(o(1), p_, pt)
                            if r:
                                mm(o(2), pt, x_)
                                ins = mm(o(3), p_, xt)
                        ins.then_inc(s_round, 1)
                for m in range(3):
                    for g, (lo_, hi_) in enumerate(GROUPS[:2]):
                        pe.wait_ge(s_E, 2 * m + g + 1)
                        pe.wait_ge(s_X, 9)
                        if m:
                            pe.wait_ge(s_T, 2 * (m - 1) + g + 1)
                        for q in range(lo_, hi_):
                            ins = mm(ps[:, 4 * g, (q - lo_) * P:(q - lo_ + 1) * P], off_diag[:, q, :], XX[:, 0, q, :])
                        ins.then_inc(s_w1, 1)
                    for g, (lo_, hi_) in enumerate(GROUPS[:2]):
                        pe.wait_ge(s_w1c, 2 * m + g + 1)
                        for q in range(lo_, hi_):
                            c_ = slice((q - lo_) * P, (q - lo_ + 1) * P)
                            if m < 2:
                                mm(ps[:, 4 * g + 2, c_], XX[:, 1, q, :], w1[:, q, :])
                            ins = mm(ps[:, 4 * g + 3, c_], w1[:, q, :], XX[:, 1, q, :])
                        ins.then_inc(s_w2, 1)
                pe.wait_ge(s_T, 6)
                for t, (lo_, hi_) in enumerate(GROUPS):
                    if t:
                        pe.wait_ge(s_S, t)
                        if t == 1:
                            for h in range(HG):
                                ins = mm(ps[:, 0, h * P:(h + 1) * P], feat(gk, 4 + h), S[:, h, :])
                        else:
                            ins = tails(0, 0, gk, lambda h: S[:, h, :])
                        ins.then_inc(s_ks, 1)
                        pe.wait_ge(s_rhs, t)
                        pe.wait_ge(s_vnc, t)
                    for q in range(lo_, hi_):
                        ins = mm(ps[:, 1, (q - lo_) * P:(q - lo_ + 1) * P], XX[:, 1, q, :], R[:, q, :])
                    ins.then_inc(s_vn, 1)
                    if t:
                        pe.wait_ge(s_oc2, t)
                    if t == 2:
                        tails(2, 0, gq, lambda h: S[:, h, :])
                    pe.wait_ge(s_vnc, t + 1)
                    for q in range(lo_, hi_):
                        o = ps[:, 2, (q - lo_) * P:(q - lo_ + 1) * P]
                        if t == 1:
                            mm(o, feat(gq, q), S[:, q - 4, :], True, False)
                        ins = mm(o, dT[:, q, :], vnew[:, q - lo_, :], t == 0, True)
                    if t < 2:
                        for q in range(lo_, hi_):
                            ins = mm(ps[:, 3, (q - lo_) * P:(q - lo_ + 1) * P], ktail[:, q, :], vnew[:, q - lo_, :])
                    ins.then_inc(s_o, 1)
                pe.wait_ge(s_on, 1)
                for q in range(9):
                    ins = pe.transpose(ps[:, 4 + q // 4, q % 4 * P:(q % 4 + 1) * P], O[:, q, :], ident[:, :])
                ins.then_inc(s_ot, 1)
                out_projection(b + AB_CHUNKS, 0)

            def cd(k, b, ready):
                for n in range(CD_CHUNKS):
                    if n >= 2:
                        pe.wait_ge(s_cdc, n - 1)
                    tiles(b + n, 2 * (n % 2), u_hi, u_lo, ready=ready if n == 0 else None)
                pe.wait_ge(s_cdc, CD_CHUNKS)
                for t, (c0, n) in enumerate(TOK):
                    pe.transpose(ps[0:n, 4, t * P:(t + 1) * P], cv[:, c0:c0 + n], ident[:, :])
                for t, (k0, _) in enumerate(SB_TILES):
                    for m in range(4):
                        ins = pe.transpose(ps[:, 5 + t, m * P:(m + 1) * P], sbv[:, m, k0:k0 + P], ident[:, :])
                ins.then_inc(s_vT, 1)
                pe.wait_ge(s_cdpad, 1)

                def half(s):
                    return slice(s * DH, (s + 1) * DH)

                def window_scores(u):
                    if u:
                        pe.wait_ge(s_wm, u)
                    for h in range(HS):
                        s_, t_ = h % 2, h // 2
                        q, kk = cq[half(s_), t_, :], kdup[half(s_), h // 4, :]
                        if u == 0:
                            ins = mm(ps[:, s_, t_ * P:(t_ + 1) * P], q[:, 0:P], kk[:, 0:P])
                        elif u == h // 4 + 1:
                            ins = mm(ps[:, h % 4, 0:2 * P], q[:, P:2 * P], kk[:, 0:2 * P])
                        elif u == 3:
                            ins = mm(ps[t_ * TAIL:(t_ + 1) * TAIL, s_, 0:T], q[:, 2 * P:TP], kk[:, 0:T])
                    ins.then_inc(s_ws, 1)

                window_scores(0)
                for u in range(UNITS):
                    n, keys = unit_shape(u)
                    if u + 1 < UNITS:
                        window_scores(u + 1)
                    pe.wait_ge(s_wp, u + 1)
                    pe.wait_ge(s_wtc, u) if u else pe.wait_ge(s_vTc, 3)
                    for m in range(n):
                        src = unit_probs(u)[:, m, :]
                        if u == 0:
                            ins = pe.transpose(ps[:, 4 + m // 4, m % 4 * P:(m % 4 + 1) * P], src, ident[:, :])
                        else:
                            for kt in range((keys + P - 1) // P):
                                w = min(P, keys - kt * P)
                                o = ps[0:w, 4 + kt, m * P:(m + 1) * P] if u < 3 else \
                                    ps[0:w, 4 + kt // 2, (2 * (kt % 2) + m) * P:(2 * (kt % 2) + m + 1) * P]
                                ins = pe.transpose(o, src[:, kt * P:kt * P + w], ident[:, :])
                    ins.then_inc(s_wt, 1)
                    pe.wait_ge(s_wtc, u + 1)
                    if u >= 2:
                        pe.wait_ge(s_woc, u - 1)
                    for h in range(HS):
                        s_, t_, g_ = h % 2, h // 2, slice(h // 4 * DH, h // 4 * DH + DH)
                        o = ps[half(s_), 6 + u % 2, :]
                        if u == 0:
                            ins = mm(o[:, t_ * P:(t_ + 1) * P], cv_tok[:, 0, g_], probsT[:, 4 * s_ + t_, :])
                        elif u == h // 4 + 1:
                            for kt in range(2):
                                ins = mm(o[:, t_ % 2 * P:(t_ % 2 + 1) * P], cv_tok[:, kt, g_],
                                         probsT[:, 4 * kt + h % 4, :], kt == 0, kt == 1)
                        elif u == 3:
                            for kt, (_, w) in enumerate(TOK):
                                ins = mm(o[:, t_ * 16:(t_ + 1) * 16], cv_tok[0:w, kt, g_],
                                         probsT[0:w, 2 * kt + s_, t_ * TAIL:t_ * TAIL + 16], kt == 0, kt == 2)
                    ins.then_inc(s_wo, 1)

                def stick_scores(x):
                    pe.wait_ge(s_zc, x) if x else pe.wait_ge(s_wm, UNITS)
                    for h in range(4 * x, 4 * x + 4):
                        off = 0
                        for k0, q0 in SB_TILES:
                            ins = mm(ps[:, h % 4, off:off + T - q0], sbk[half(h % 2), h // 2, k0:k0 + P],
                                     sbq[half(h % 2), h // 2, q0:T])
                            off += T - q0
                    ins.then_inc(s_z, 1)

                stick_scores(0)
                offs = [0, T, 2 * T - P]
                for x in range(2):
                    if x == 0:
                        stick_scores(1)
                    pe.wait_ge(s_lm, x + 1)
                    pe.wait_ge(s_soc, x) if x else pe.wait_ge(s_woc, UNITS)
                    for h in range(4):
                        for j, (k0, q0) in enumerate(SB_TILES):
                            for i in range(j, 3):
                                q1 = SB_TILES[i][1]
                                ins = mm(ps[:, 4 + h, offs[j] + q1 - q0:offs[j] + T - q0],
                                         masks[:, LOWER, :] if i == j else ones[:, :],
                                         lm[:, h, offs[i]:offs[i] + T - q1], i == j, i == 2)
                    ins.then_inc(s_cum, 1)
                    pe.wait_ge(s_am, x + 1)
                    for h in range(4 * x, 4 * x + 4):
                        for j, (k0, q0) in enumerate(SB_TILES):
                            ins = mm(ps[half(h % 2), 4 + h // 2 % 2, q0:T], sbv_tok[:, j, h * DH:(h + 1) * DH],
                                     zs[:, h % 4, offs[j]:offs[j] + T - q0], j == 0, j == 2)
                    ins.then_inc(s_so, 1)
                out_projection(b + CD_CHUNKS, 2)

            pe.wait_ge(s_const, 16)
            pe.wait_ge(s_in, 80)
            for g in range(2):
                for t, n in enumerate((P, P, N_META)):
                    for m in range(4):
                        src = x_tok[0:n, t, (4 * g + m) * P:(4 * g + m + 1) * P]
                        ins = pe.transpose(ps[:, XB + 2 * t + g, m * n:(m + 1) * n], src, ident[0:n, 0:n])
                    ins.then_inc(s_xT, 1)
            pe.transpose(ps[:, 0, 0:12 * KD], g_tok[:, :], ident[0:12 * KD, 0:12 * KD]).then_inc(s_gT, 1)
            pe.transpose(ps[:, 1, 0:4 * 12], cw_tok[:, :], ident[0:4 * 12, 0:4 * 12]).then_inc(s_cwT, 1)
            pe.wait_ge(s_ones, 1)
            pe.wait_ge(s_cwc, 1)
            for k, (kind, b, layer, f) in enumerate(subs):
                pre_norm_sum(k)

                def ready(kk):
                    pe.wait_ge(s_ulo, KD * k + kk + 1)

                if kind == "ffn":
                    pair(b, f, 0, ready=ready)
                    with pe.Fori(0, (NPAIR - 3) // 2) as i:
                        pair(b, f, 1, i)
                        pair(b, f, 2, i)
                    pair(b, f, NPAIR - 2)
                    pair(b, f, NPAIR - 1)
                    for blk in range(NBLK):
                        for half in range(2):
                            pe.wait_ge(s_hid, 2 + NPAIR * f + NPAIR - 1 + half)
                            h = slice(half * KH, (half + 1) * KH)
                            tiles(b + 2 * NPAIR + 2 * blk + half, 2 * blk, hid_hi[:, h, :], hid_lo[:, h, :],
                                  first=half == 0, last=half == 1)
                elif kind == "ab":
                    ab(k, b, ready)
                else:
                    cd(k, b, ready)
                post_norm_sum(k)
            for t in range(2):
                for g in range(2):
                    pe.wait_ge(s_h, KD // 2 * len(subs) + 2 * g + 2)
                    for m in range(4):
                        src = hT[:, 4 * g + m, N_META + t * P:N_META + (t + 1) * P]
                        ins = pe.transpose(ps[:, 2 + 2 * t + g, m * P:(m + 1) * P], src, ident[:, :])
                    ins.then_inc(s_oT, 1)


INPUTS = ["x", "meta_tokens", "norm_gains", "ffn_w_gate", "ffn_w_up", "ffn_w_down", "ab_w_in", "ab_conv_w",
          "ab_a_log", "ab_dt_bias", "ab_out_norm", "ab_w_out", "cd_w_in", "cd_sinks", "cd_w_out"]


def kernel(**inputs):
    import concourse.bacc as bacc
    from concourse.bass_utils import run_bass_kernel_spmd

    nc = bacc.Bacc("TRN2", target_bir_lowering=False, num_devices=1)
    tables = shape_constants()
    arrays = {name: np.ascontiguousarray(inputs[name]) for name in INPUTS} | tables
    aps = {name: nc.dram_tensor(name, v.shape, mybir.dt.from_np(v.dtype), kind="ExternalInput").ap()
           for name, v in arrays.items()}
    out = nc.dram_tensor("out", (1, SEQ, D), F32, kind="ExternalOutput").ap()
    build(nc, aps, {name: aps[name] for name in tables}, out)
    return run_bass_kernel_spmd(nc, [arrays], core_ids=[0]).results[0]["out"]
```

```python
from contextlib import ExitStack

import concourse.bass as bass
from concourse import mybir
import numpy as np
F32 = mybir.dt.float32
F32R = mybir.dt.float32r
ALU = mybir.AluOpType
ACT = mybir.ActivationFunctionType
AX = mybir.AxisListType

P = 128
N_META = 16
SEQ = 256
T = N_META + SEQ
D = 1024
KD = D // P
FF = 2816
KF = FF // P
EPS = 1e-6
CB = 256
KH = KF // 2
RAW = KH * CB
NRAW = 4
NW = 2
NPAIR = FF // CB
NBLK = D // CB
BANK = 512
LN_HALF = float(np.log(0.5))
LN_QSCALE = float(-0.5 * np.log(128.0))

EXP_SET = "natural_log_exp_and_others"
SILU_SET = "silu_and_others"

AB_IN = 4104
CD_IN = 2304
AB_CHUNKS = AB_IN // CB
CD_CHUNKS = CD_IN // CB

SUBLAYERS = [("ffn", 0), ("ab", 0), ("ffn", 0), ("ffn", 1), ("cd", 1), ("ffn", 1)]
SIZES = {"ffn": 2 * NPAIR + 2 * NBLK, "ab": AB_CHUNKS + NBLK, "cd": CD_CHUNKS + NBLK}

HR = HG = 4
TAIL = 32
TP = 2 * P + TAIL
N_MASKS = 8
UPPER, UPPER32, LOWER, LOWER32, DIAG16, MERGE = 0, 1, 2, 3, 4, 5
TOK = [(0, P), (P, P), (2 * P, T - 2 * P)]

AB_FIRST = {"rq": 0, "rk": 512, "rv": 1024, "rg": 1536, "gq": 2048, "gk": 2560, "gv": 3072, "gz": 3584}
AB_ROLE = [("rq", 0), ("rq", 1), ("rk", 0), ("rk", 1), ("rv", 0), ("rv", 1), ("gk", 0), ("rg", 0),
           ("gk", 1), ("rg", 1), ("gq", 0), ("gz", 0), ("gq", 1), ("gz", 1), ("gv", 0), ("gv", 1)]
AB_CONV = [n for n, (what, _) in enumerate(AB_ROLE) if what in ("gq", "gk", "gv")]
AB_GATES = [n for n, (what, _) in enumerate(AB_ROLE) if what in ("rg", "gz")]
AB_ROT, AB_V = range(0, 4), range(4, 6)

HS, DH = 8, 64
WINDOW = 128
NEG = -1e30
SB_TILES = [(0, 0), (P, P), (T - P, 2 * P)]
SBW = sum(T - q0 for _, q0 in SB_TILES)
CD_ORDER = [3, 5, 4, 6, 2, 0, 1, 7, 8]


def shape_constants():
    c = {}
    c["c_ident"] = np.eye(P, dtype=np.float32)
    i, j = np.arange(P)[:, None], np.arange(P)[None, :]
    masks = np.zeros((P, N_MASKS, P), np.float32)
    masks[:, UPPER] = i <= j
    masks[:, UPPER32] = (i <= j) & (i // TAIL == j // TAIL)
    masks[:, LOWER] = i > j
    masks[:, LOWER32] = (i > j) & (i // TAIL == j // TAIL)
    masks[:, DIAG16] = -1.0 * (i // 16 == j // 16)
    for n, size in enumerate((16, 32, 64)):
        masks[:, MERGE + n] = (i // (2 * size) == j // (2 * size)) & (j // size == i // size + 1)
    c["c_masks"] = masks
    swap = np.zeros((P, P), np.float32)
    swap[np.arange(1, P, 2), np.arange(0, P, 2)] = -1.0
    swap[np.arange(0, P, 2), np.arange(1, P, 2)] = 1.0
    c["c_swap"] = swap
    inv_freq = (1.0 / (np.float32(10000.0) ** np.linspace(0.0, 1.0, P // 2, dtype=np.float32))).astype(np.float32)
    ang = np.repeat(inv_freq, 2)[:, None] * np.arange(T, dtype=np.float32)[None, :]
    c["c_rope"] = np.stack([np.cos(ang), np.sin(ang)], axis=1).astype(np.float32)
    gamma = np.log1p(-np.exp2(-5.0 - np.arange(HR, dtype=np.float64)))[None, :, None]
    diff = (np.arange(T)[None, None, :] - np.arange(P)[:, None, None]).astype(np.float64)
    c["c_decay"] = (np.where(diff >= 0, np.exp(np.maximum(diff, 0) * gamma), 0.0) * P ** -0.5).astype(np.float32)
    key, q = np.arange(T)[None, None, :], np.arange(P)[:, None, None] + P * np.arange(3)[None, :, None]
    q = np.where(q < 2 * P, q, 2 * P + q % TAIL)
    sees = (key <= q) & ((key < N_META) | (q - key < WINDOW)) | (q >= T)
    c["c_window"] = np.where(sees, 0.0, NEG).astype(np.float32)
    c["c_before"] = np.concatenate([(k0 + np.arange(P)[:, None] < np.arange(q0, T)[None, :])
                                    & (k0 + np.arange(P)[:, None] >= q0) for k0, q0 in SB_TILES], axis=1).astype(np.float32)
    c["c_head_of"] = (i[:, 0:1] // TAIL == np.arange(HG)[None, :]).astype(np.float32)
    return c


class Steps:

    def __init__(self, engine, sem):
        self.engine, self.sem, self.n, self.loop = engine, sem, 0, 0

    def done(self, ins):
        ins.then_inc(self.sem, 1)
        self.n += 1
        self.engine.wait_ge(self.sem, self.n + self.loop)

    def enter(self, i, steps):
        self.loop, self.until = i * steps, self.n + steps

    def leave(self, steps, count):
        assert self.n == self.until
        self.n += steps * (count - 1)
        self.loop = 0


def build(nc, a, c, out):
    ctx = ExitStack()
    place = [nc.sbuf_base + (-nc.sbuf_base) % 64]

    def at(name, shape, dtype, where):
        return nc.alloc_sbuf_tensor_at(name, shape, dtype, offset=where)

    def sb(name, free, dtype=F32, parts=P):
        size = 4
        for n in free:
            size *= n
        t = at(name, [parts, *free], dtype, place[0])
        place[0] += size + (-size) % 64
        return t

    def sem(name):
        return ctx.enter_context(nc.semaphore(name))

    with ctx:
        raw = sb("raw", [NRAW, RAW])
        w_hi = sb("w_hi", [NW, RAW], F32R)
        w_lo = sb("w_lo", [NW, RAW], F32R)
        hT = sb("hT", [KD, T])
        yT = sb("yT", [KD, T])
        u_hi = sb("u_hi", [KD, T], F32R)
        u_lo = sb("u_lo", [KD, T], F32R)
        ss = sb("ss", [T])
        lnv = sb("lnv", [T])
        rstd = sb("rstd", [2, T])
        ident = sb("ident", [P])
        ones = sb("ones", [P])
        gains = sb("gains", [12 * KD])
        masks = sb("masks", [N_MASKS, P])
        swap = sb("swap", [P])
        head_of = sb("head_of", [HG])
        convw = sb("convw", [4 * 12])
        w_ba = sb("w_ba", [KD, 2 * HG])
        dt4 = sb("dt4", [HG])
        alog4 = sb("alog4", [HG])
        out_norm = sb("out_norm", [1])
        scratch = place[0]
        gates = sb("gates", [2, 2, T])
        prod = sb("prod", [2, 2, T])
        y_sq = sb("y_sq", [2, 2, T])
        h_sq = sb("h_sq", [KD // 2, 2, T])
        arena = place[0]
        hid_hi = at("hid_hi", [P, KF, T], F32R, arena)
        hid_lo = at("hid_lo", [P, KF, T], F32R, arena + KF * T * 4)
        x_tok = at("x_tok", [P, 3, D], F32, arena)
        g_tok = at("g_tok", [12 * KD, P], F32, arena + 3 * D * 4)
        o_tok = at("o_tok", [P, 2, D], F32, arena)
        cw_tok = at("cw_tok", [4 * 12, P], F32, arena + 3 * D * 4 + P * 4)
        assert arena + 2 * KF * T * 4 <= nc.sbuf_usable_end

        place[0] = scratch
        gq = sb("gq", [HG, TP])
        gk = sb("gk", [HG, TP])
        gv = sb("gv", [HG, TP])
        gz = sb("gz", [HG, T])
        ba = sb("ba", [3, 2 * HG])
        beta9 = sb("beta9", [9])
        g9 = sb("g9", [9])
        gc9 = sb("gc9", [9])
        small = sb("small", [8, 3 * HG])
        r9 = sb("r9", [9])
        gdn_place = place[0]
        rope = sb("rope", [2, T])
        decay = sb("decay", [HR, T])
        rq = sb("rq", [HR, T])
        rk = sb("rk", [HR, T])
        rv = sb("rv", [HR, T])
        rg = sb("rg", [HR, T])
        cacc = sb("cacc", [2, 2, T])
        qraw = sb("qraw", [2, T])
        rot = sb("rot", [2, T])
        l2sq = sb("l2sq", [HG, T])
        rv_tok = sb("rv_tok", [3, HR * P])
        attn = sb("attn", [HR, T + T - P + 16])
        ret = sb("ret", [HR, T])
        l2r = raw[:, :, KD * CB:KD * CB + T]
        assert place[0] <= nc.sbuf_usable_end
        place[0] = gdn_place
        dmat = sb("dmat", [9, P])
        dT = sb("dT", [9, P])
        dN = sb("dN", [9, P])
        eG = sb("eG", [9, P])
        PP = sb("PP", [2, 9, P])
        XX = sb("XX", [2, 9, P])
        R = sb("R", [9, P])
        ktail = sb("ktail", [8, P])
        vnew = sb("vnew", [HG, P])
        S = sb("S", [HG, P])
        vtmp = sb("vtmp", [HG, P])
        assert place[0] <= nc.sbuf_usable_end
        off_diag = eG
        w1 = dN
        O = gv[:, :, :].rearrange("p h t -> p (h t)").rearrange("p (n c) -> p n c", c=P)

        place[0] = scratch
        sbq = sb("sbq", [HS // 2, T])
        sbk = sb("sbk", [HS // 2, T])
        sbv = sb("sbv", [HS // 2, T])
        cq = sb("cq", [HS // 2, TP])
        kdup = sb("kdup", [2, T])
        cv = sb("cv", [T])
        window = sb("window", [3, T])
        before = sb("before", [SBW])
        sinks8 = sb("sinks8", [2, HS])
        sinks2 = sb("sinks2", [2])
        cv_tok = sb("cv_tok", [3, P])
        sbv_tok = sb("sbv_tok", [3, HS * DH])
        probs = sb("probs", [2, 4 * TP])
        probsT = sb("probsT", [8, P])
        wmx = sb("wmx", [2, 4, 8])
        zs = [sb("zs", [4, SBW]), raw[:, :, KD * CB:KD * CB + SBW]]
        lb = [sb("lb_0", [4, SBW]), sb("lb_1", [4, SBW])]
        lm = [sb("lm", [4, SBW]),
              yT[:, :, :].rearrange("p m t -> p (m t)")[:, 0:4 * SBW].rearrange("p (h c) -> p h c", c=SBW)]
        assert place[0] <= nc.sbuf_usable_end

        ps = ctx.enter_context(nc.psum_tensor("ps", [P, 8, BANK], F32))

        s_in = sem("inputs_loaded")
        s_const = sem("constants_loaded")
        s_ones = sem("ones_set")
        s_gT = sem("gains_transposed")
        s_gains = sem("gains_ready")
        s_xT = sem("input_transposed")
        s_xc = sem("input_middle_copied")
        s_raw = [sem(f"raw_loaded_{i}") for i in range(NRAW)]
        s_hi = sem("hi_split")
        s_lo = sem("lo_split")
        s_used = sem("chunk_used")
        s_silu = sem("silu_ready")
        s_hid = sem("hidden_ready")
        s_prod = sem("hidden_product_ready")
        s_hhi = sem("hidden_hi_ready")
        s_gs = sem("gate_scaled")
        s_ytile = sem("last_output_tile_but_one")
        s_ysq0 = sem("first_tile_squared")
        s_ysq = sem("y_squared")
        s_ss = sem("y_squares_added")
        s_ysum = sem("y_sum_ready")
        s_yr = sem("y_groups_scaled")
        s_h = sem("h_group_ready")
        s_hsq = sem("h_squared")
        s_hadd = sem("h_squares_added")
        s_hsum = sem("h_squares_summed")
        s_pool = sem("pool_step")
        s_rstd = sem("rstd_ready")
        s_uhi = sem("u_hi_ready")
        s_ulo = sem("u_lo_ready")
        s_act = sem("act_step")
        s_dve = sem("dve_step")
        s_oT = sem("output_transposed")
        s_oa = sem("first_output_tile_copied")
        s_oc = sem("second_output_tile_copied")
        s_out = sem("output_stored")

        s_cwT = sem("conv_weights_transposed")
        s_cwc = sem("conv_weights_copied")
        s_tab = sem("ab_tables_loaded")
        s_pads = sem("ab_pads_zeroed")
        s_wba = sem("ba_weights_scaled")
        s_ba = sem("ba_projected")
        s_bac = sem("ba_copied")
        s_cx = sem("conv_input_ready")
        s_tap = sem("conv_first_tap")
        s_conv = sem("conv_done")
        s_csilu = sem("conv_silu_done")
        s_evac = sem("ab_chunk_copied")
        s_gsilu = sem("ab_gate_silu_done")
        s_swap = sem("pairs_swapped")
        s_rot = sem("rotated")
        s_l2sq = sem("l2_squared")
        s_l2sum = sem("l2_summed")
        s_l2r = sem("l2_root_ready")
        s_l2 = sem("l2_normed")
        s_rvT = sem("ret_v_transposed")
        s_rvc = sem("ret_v_copied")
        s_score = sem("ret_scores")
        s_attn = sem("ret_scores_decayed")
        s_pv = sem("ret_out")
        s_ret = sem("ret_out_copied")
        s_mean = sem("ret_mean")
        s_cent = sem("ret_centered")
        s_rsq = sem("ret_squared")
        s_var = sem("ret_var")
        s_rrt = sem("ret_root_ready")
        s_m32 = sem("mixed32_ready")
        s_mhi = sem("mixed_hi_ready")
        s_mlo = sem("mixed_lo_ready")
        s_x = sem("decay_input_ready")
        s_xe = sem("decay_exps_ready")
        s_g9 = sem("g_beta_ready")
        s_gsum = sem("g_cumulated")
        s_dcl = sem("decay_exponents_ready")
        s_dexp = sem("decays_ready")
        s_dN = sem("beta_decay_ready")
        s_kT = sem("k_transposed")
        s_ktail = sem("k_tail_ready")
        s_kk = sem("kk_qk_ready")
        s_A = sem("A_ready")
        s_AT = sem("A_transposed")
        s_ATc = sem("A_transposed_copied")
        s_PP0 = sem("first_power_ready")
        s_gdec = sem("gdn_qk_decayed")
        s_R = sem("beta_v_ready")
        s_X0 = sem("inverse_started")
        s_IP = sem("last_factor_ready")
        s_round = sem("doubling_products")
        s_P = sem("power_copied")
        s_X = sem("inverse_doubled")
        s_E = sem("off_diagonal_ready")
        s_w1 = sem("merge_first_product")
        s_w1c = sem("merge_first_copied")
        s_w2 = sem("merge_products")
        s_T = sem("merge_done")
        s_ks = sem("k_state_ready")
        s_rhs = sem("rhs_ready")
        s_vn = sem("v_new_ready")
        s_vnc = sem("v_new_copied")
        s_o = sem("gdn_out")
        s_oc2 = sem("gdn_out_copied")
        s_S = sem("state_ready")
        s_osq = sem("gdn_out_squared")
        s_oss = sem("gdn_out_summed")
        s_ort = sem("gdn_out_root")
        s_on = sem("gdn_out_normed")
        s_ot = sem("gdn_out_transposed")

        s_cdtab = sem("cd_tables_loaded")
        s_cdpad = sem("cd_pads_zeroed")
        s_cdc = sem("cd_chunk_copied")
        s_vT = sem("cd_v_transposed")
        s_vTc = sem("cd_v_copied")
        s_ws = sem("window_scores")
        s_wst = sem("window_scores_read")
        s_wm = sem("window_max_ready")
        s_we = sem("window_exps_ready")
        s_wp = sem("window_probs_ready")
        s_wt = sem("window_probs_transposed")
        s_wtc = sem("window_probsT_copied")
        s_wo = sem("window_out")
        s_woc = sem("window_out_copied")
        s_z = sem("stick_scores")
        s_zc = sem("stick_scores_copied")
        s_sp = sem("stick_softplus_ready")
        s_lm = sem("stick_logs_ready")
        s_cum = sem("stick_cumulated")
        s_aw = sem("stick_exponents_ready")
        s_ae = sem("stick_exps_ready")
        s_am = sem("stick_weights_ready")
        s_so = sem("stick_out")
        s_soc = sem("stick_out_copied")

        block = ctx.enter_context(nc.Block())

        UNITS = 4

        def unit_shape(u):
            return ((8, P), (4, 2 * P), (4, 2 * P), (2, T))[u]

        def unit_scores(u):
            if u == 0:
                return [(4 * z, ps[:, z, :].rearrange("p (n c) -> p n c", c=P)) for z in range(2)]
            n, keys = unit_shape(u)
            return [(0, ps[:, 0:n, 0:keys])]

        def unit_probs(u):
            n, keys = unit_shape(u)
            return probs[:, u % 2, 0:n * keys].rearrange("p (n c) -> p n c", c=keys)

        GROUPS = ((0, 4), (4, 8), (8, 9))

        def blocks(bank, lo_, hi_):
            return ps[:, bank, 0:(hi_ - lo_) * P].rearrange("p (n c) -> p n c", c=P)

        def over(col, shape):
            return col.unsqueeze(2).to_broadcast(shape)

        def mask(n, count):
            return masks[:, n:n + 1, :].to_broadcast([P, count, P])

        subs, n, f = [], 0, 0
        for kind, layer in SUBLAYERS:
            subs.append((kind, n, layer, f))
            n += SIZES[kind]
            f += kind == "ffn"
        n_chunks = n

        def rows(n):
            for kind, b, _, _ in subs:
                if b <= n < b + SIZES[kind]:
                    return KH if kind == "ffn" and n - b >= 2 * NPAIR else KD

        def gain(layer, s, m):
            g = (layer * 6 + s) * KD + m
            return gains[:, g:g + 1]

        def norm_of(k):
            return 2 * (k % 3)

        def sum_bank(kind):
            return {"ffn": 1, "ab": 6, "cd": 7}[kind]

        def tokens(k):
            return slice(N_META if k == len(subs) - 1 else 0, T)

        def out_tokens(k):
            return slice(N_META if k >= len(subs) - 2 else 0, T)

        def rstd_two(slot, tok=slice(0, T)):
            return rstd[:, slot:slot + 1, tok].to_broadcast([P, 2, tok.stop - tok.start])

        def two(b, tok=slice(0, T)):
            return ps[:, b:b + 2, tok]

        def pair_banks(j):
            return 4 - 4 * (j % 2)

        ffn_tokens = [tokens(k) for k, (kind, _, _, _) in enumerate(subs) if kind == "ffn"]

        def block_at(kind, i):
            return {"ffn": (0, 1, 2, 3), "ab": (2, 3, 0, 1), "cd": (0, 2, 1, 3)}[kind][i]

        XB = 2

        @block.sync
        def _(sp):
            sp.dma_start(ident[:, :], c["c_ident"]).then_inc(s_const, 16)
            sp.dma_start(x_tok[:, 0, :], a["x"][0, 0:P, :]).then_inc(s_in, 16)
            sp.dma_start(x_tok[:, 1, :], a["x"][0, P:2 * P, :]).then_inc(s_in, 16)
            sp.dma_start(x_tok[0:N_META, 2, :], a["meta_tokens"]).then_inc(s_in, 16)
            sp.dma_start(cw_tok[:, :], a["ab_conv_w"][0].rearrange("k (m p) -> (k m) p", p=P)).then_inc(s_in, 16)
            sp.dma_start(g_tok[:, :], a["norm_gains"].rearrange("l s (m p) -> (l s m) p", p=P)).then_inc(s_in, 16)

            def load(n, src, i=0):
                sp.wait_ge(s_lo, n + 1 + i * NRAW)
                dst = raw[:, n % NRAW, 0:rows(n) * CB].rearrange("p (k c) -> p k c", c=CB)
                sp.dma_start(dst, src).then_inc(s_raw[n % NRAW], 16)

            for k, (kind, b, layer, f) in enumerate(subs):
                if kind == "ffn":
                    wg = a["ffn_w_gate"][layer, f % 2].rearrange("(k p) c -> p k c", p=P)
                    wu = a["ffn_w_up"][layer, f % 2].rearrange("(k p) c -> p k c", p=P)
                    wd = a["ffn_w_down"][layer, f % 2].rearrange("(k p) c -> p k c", p=P)
                    with sp.Fori(0, NPAIR // 2) as i:
                        for t in range(2):
                            load(b + 2 * t, wg[:, :, bass.ds(i * 2 * CB + t * CB, CB)], i)
                            load(b + 2 * t + 1, wu[:, :, bass.ds(i * 2 * CB + t * CB, CB)], i)
                    if k == 0:
                        for dst, src in ((masks[:, :, :], c["c_masks"]), (swap[:, :], c["c_swap"]),
                                         (head_of[:, :], c["c_head_of"]),
                                         (w_ba[:, :, :], a["ab_w_in"][0, :, AB_CHUNKS * CB:AB_IN].rearrange(
                                             "(k p) c -> p k c", p=P)),
                                         (dt4[:, :], a["ab_dt_bias"].to_broadcast([P, HG])),
                                         (alog4[:, :], a["ab_a_log"].to_broadcast([P, HG])),
                                         (out_norm[:, :], a["ab_out_norm"].rearrange("o p -> p o"))):
                            sp.dma_start(dst, src).then_inc(s_const, 16)
                    load(b + 2 * NPAIR - 2, wg[:, :, FF - CB:FF])
                    load(b + 2 * NPAIR - 1, wu[:, :, FF - CB:FF])
                    for blk in range(NBLK):
                        for half in range(2):
                            load(b + 2 * NPAIR + 2 * blk + half,
                                 wd[:, half * KH:(half + 1) * KH, blk * CB:(blk + 1) * CB])
                if kind == "ab":
                    w_in = a["ab_w_in"][0].rearrange("(k p) c -> p k c", p=P)
                    w_out = a["ab_w_out"][0].rearrange("(k p) c -> p k c", p=P)
                    for n, (what, m) in enumerate(AB_ROLE):
                        c0 = AB_FIRST[what] + m * CB
                        load(b + n, w_in[:, :, c0:c0 + CB])
                        if n == 4:
                            sp.wait_ge(s_used, NW + b + 1)
                            sp.wait_ge(s_hsum, k + 1)
                            sp.dma_start(rope[:, :, :], c["c_rope"]).then_inc(s_tab, 16)
                            sp.dma_start(decay[:, :, :], c["c_decay"]).then_inc(s_tab, 16)
                    for i in range(NBLK):
                        c0 = block_at("ab", i) * CB
                        load(b + AB_CHUNKS + i, w_out[:, :, c0:c0 + CB])
                if kind == "cd":
                    w_in = a["cd_w_in"][0].rearrange("(k p) c -> p k c", p=P)
                    w_out = a["cd_w_out"][0].rearrange("(k p) c -> p k c", p=P)
                    for n in range(CD_CHUNKS):
                        load(b + n, w_in[:, :, CD_ORDER[n] * CB:(CD_ORDER[n] + 1) * CB])
                        if n == 4:
                            sp.wait_ge(s_used, NW + b + 1)
                            sp.wait_ge(s_hsum, k + 1)
                            sp.dma_start(window[:, :, :], c["c_window"]).then_inc(s_cdtab, 16)
                            sp.dma_start(before[:, :], c["c_before"]).then_inc(s_cdtab, 16)
                            sp.dma_start(sinks8[:, 1, :], a["cd_sinks"].to_broadcast([P, HS])).then_inc(s_cdtab, 16)
                            for h in range(4):
                                sp.dma_start(sinks2[h * TAIL:(h + 1) * TAIL, :],
                                             a["cd_sinks"][:, 2 * h:2 * h + 2].to_broadcast([TAIL, 2])).then_inc(s_cdtab, 16)
                    for i in range(NBLK):
                        c0 = block_at("cd", i) * CB
                        load(b + CD_CHUNKS + i, w_out[:, :, c0:c0 + CB])
            for g in range(2):
                cols = slice(g * BANK, (g + 1) * BANK)
                for t, copied in enumerate((s_oa, s_oc)):
                    sp.wait_ge(copied, g + 1)
                    sp.dma_start(out[0, t * P:(t + 1) * P, cols], o_tok[:, t, cols]).then_inc(s_out, 16)
            sp.wait_ge(s_out, 64)

        @block.gpsimd
        def _(pool):
            step = Steps(pool, s_pool)
            pool.memset(ones[:, :], 1.0).then_inc(s_ones, 1)

            def scale_y(k):
                pool.wait_ge(s_rstd, 2 * k)
                for g in (2, 3):
                    m, tok = slice(2 * g, 2 * g + 2), out_tokens(k - 1)
                    pool.tensor_tensor(yT[:, m, tok], yT[:, m, tok], rstd_two(0, tok), ALU.mult).then_inc(s_yr, 1)

            for k, (kind, b, _, _) in enumerate(subs):
                if k:
                    scale_y(k)
                pool.wait_ge(s_lo, NRAW + b + 1)
                pool.wait_ge(s_hi, b + 2)
                cols = slice(0, KD * CB)
                pool.tensor_tensor(w_lo[:, (b + 1) % NW, cols], raw[:, (b + 1) % NRAW, cols],
                                   w_hi[:, (b + 1) % NW, cols].bitcast(F32), ALU.subtract).then_inc(s_lo, 1)
                for g in range(1, KD // 2):
                    pool.wait_ge(s_hsq, KD // 2 * k + g + 1)
                    step.done(pool.tensor_tensor(h_sq[:, 0, :, :], h_sq[:, 0, :, :], h_sq[:, g, :, :], ALU.add))
                pool.tensor_tensor(h_sq[:, 0, 0, :], h_sq[:, 0, 0, :], h_sq[:, 0, 1, :], ALU.add).then_inc(s_hadd, 1)
                if kind == "ab":
                    pool.wait_ge(s_used, NW + b + 1)
                    pool.wait_ge(s_hsum, k + 1)
                    for t in (gq, gk, gv):
                        pool.memset(t[:, :, T:TP], 0.0).then_inc(s_pads, 1)
                    pool.memset(ba[:, :, :], 0.0).then_inc(s_pads, 1)
                    pool.wait_ge(s_const, 16 * 8)
                    pool.wait_ge(s_g9, 1)
                    pool.wait_ge(s_dexp, 4)
                    pool.tensor_tensor(dN[:, 0:8, :], dmat[:, 0:8, :], mask(LOWER, 8), ALU.mult)
                    step.done(pool.tensor_tensor(dN[:, 8, :], dmat[:, 8, :], masks[:, LOWER32, :], ALU.mult))
                    pool.tensor_tensor(dN[:, :, :], dN[:, :, :], over(beta9[:, :], [P, 9, P]), ALU.mult).then_inc(s_dN, 1)
                    pool.wait_ge(s_A, 1)
                    pool.tensor_tensor(PP[:, 0, :, :], dN[:, :, :], mask(DIAG16, 9), ALU.mult).then_inc(s_PP0, 1)
                    pool.wait_ge(s_kk, 2)
                    for t in (gq, gk):
                        pool.tensor_tensor(t[:, :, P:2 * P], t[:, :, P:2 * P], eG[:, 4:8, :], ALU.mult)
                        pool.tensor_tensor(t[:, :, 2 * P:TP], t[:, :, 2 * P:TP],
                                           eG[:, 8, :].rearrange("p (h t) -> p h t", t=TAIL), ALU.mult)
                    pool.tensor_copy(small[:, 0, 0:HG].unsqueeze(2), eG[:, 4:8, P - 1:P]).then_inc(s_gdec, 1)
                if kind == "cd":
                    pool.wait_ge(s_used, NW + b + 1)
                    pool.wait_ge(s_hsum, k + 1)
                    pool.memset(cq[:, :, T:TP], 0.0).then_inc(s_cdpad, 1)
                    pool.wait_ge(s_cdtab, 16 * 7)
                    for x in range(2):
                        pool.wait_ge(s_ae, x + 1)
                        pool.tensor_tensor(zs[x][:, :, :], zs[x][:, :, :],
                                           before[:, :].unsqueeze(1).to_broadcast([P, 4, SBW]), ALU.mult).then_inc(s_am, 1)
            scale_y(len(subs))

        @block.scalar
        def _(act):
            step = Steps(act, s_act)

            def hi(n, i=0):
                if n >= n_chunks:
                    return
                act.wait_ge(s_raw[n % NRAW], 16 * (n // NRAW + 1) + i * 16)
                act.wait_ge(s_used, n + 1 + i * 4)
                act.activation(w_hi[:, n % NW, 0:rows(n) * CB], raw[:, n % NRAW, 0:rows(n) * CB], ACT.Copy)\
                    .then_inc(s_hi, 1)

            def silu(f, j, i=0):
                act.wait_ge(s_gs, NPAIR * f + j + 1 + i * 2)
                g = gates[:, j % 2, :, ffn_tokens[f]]
                act.activation(g, g, ACT.Silu).then_inc(s_silu, 1)

            def hidden_hi(f, j, i=0):
                act.wait_ge(s_prod, 2 + NPAIR * f + j + 1 + i * 2)
                tok = ffn_tokens[f]
                act.activation(hid_hi[:, bass.ds(i * 4 + 2 * j, 2), tok], prod[:, j % 2, :, tok], ACT.Copy)\
                    .then_inc(s_hhi, 1)

            def y_block(k, i, n):
                q, layer, blk = NBLK * k + i, subs[k][2], block_at(subs[k][0], i)
                if q >= 2:
                    act.wait_ge(s_ss, q - 1)
                last, tok = i == NBLK - 1, out_tokens(k)
                if last:
                    act.wait_ge(s_ytile, k + 1)
                    act.activation(y_sq[:, q % 2, 0, tok], ps[:, 2 * blk, tok], ACT.Square).then_inc(s_ysq0, 1)
                    act.activation(yT[:, 2 * blk, tok], ps[:, 2 * blk, tok], ACT.Copy,
                                   scale=gain(layer, norm_of(k) + 1, 2 * blk))
                act.wait_ge(s_used, NW + n + 1)
                if last:
                    act.activation(y_sq[:, q % 2, 1, tok], ps[:, 2 * blk + 1, tok], ACT.Square).then_inc(s_ysq, 1)
                else:
                    act.activation(y_sq[:, q % 2, :, tok], two(2 * blk, tok), ACT.Square).then_inc(s_ysq, 1)
                for m in range(2 * blk + last, 2 * blk + 2):
                    act.activation(yT[:, m, tok], ps[:, m, tok], ACT.Copy, scale=gain(layer, norm_of(k) + 1, m))

            def inverse_root(slot, bank, log_scale, tok=slice(0, T)):
                step.done(act.activation(lnv[:, tok], ps[:, bank, tok], ACT.Ln, bias=EPS, scale=1.0 / D))
                act.activation(rstd[:, slot, tok], lnv[:, tok], ACT.Exp, bias=log_scale, scale=-0.5).then_inc(s_rstd, 1)

            def post_norm(k, kind):
                act.wait_ge(s_ysum, k + 1)
                inverse_root(0, 0, LN_HALF if kind == "ffn" else 0.0, out_tokens(k))

            def pre_norm(k, kind, layer, b):
                for g in range(KD // 2):
                    act.wait_ge(s_h, KD // 2 * k + g + 1)
                    for m in (2 * g, 2 * g + 1):
                        act.activation(u_hi[:, m, :], hT[:, m, :], ACT.Copy, scale=gain(layer, norm_of(k), m))\
                            .then_inc(s_uhi, 1)
                    act.activation(h_sq[:, g, :, :], hT[:, 2 * g:2 * g + 2, :], ACT.Square).then_inc(s_hsq, 1)
                hi(b + 2)
                act.wait_ge(s_hsum, k + 1)
                inverse_root(1, sum_bank(kind), 0.0)

            def split_hi(half):
                act.wait_ge(s_m32, half + 1)
                if half == 0:
                    act.wait_ge(s_used, NW + subs[1][1] + AB_CHUNKS)
                m = slice(4 * (half % 2), 4 * (half % 2) + 4)
                act.activation(u_hi[:, m, :], yT[:, m, :], ACT.Copy).then_inc(s_mhi, 1)

            def out_projection(k, b):
                for blk in range(NBLK):
                    hi(b + blk + 2) if blk < 3 else None
                    y_block(k, blk, b + blk)

            def ab(k, b):
                act.preload_act_table_set(SILU_SET)
                to = {"rg": rg, "gz": gz, "gq": gq, "gk": gk, "gv": gv}

                def l2_square(v, x, m, count):
                    act.wait_ge(s_csilu, (1, 2, 4)[v])
                    act.activation(l2sq[:, 0:count, :], x[:, m:m + count, 0:T], ACT.Square).then_inc(s_l2sq, 1)

                def l2_root(v, count):
                    act.wait_ge(s_l2sum, v + 1)
                    if v:
                        act.wait_ge(s_l2, v)
                    o = ps[:, 0:4, 0:T] if v == 2 else ps[:, 4:6, 0:T]
                    step.done(act.activation(l2r[:, 0:count, :], o, ACT.Ln, bias=EPS))
                    act.activation(l2r[:, 0:count, :], l2r[:, 0:count, :], ACT.Exp, scale=-0.5,
                                   bias=LN_QSCALE if v == 2 else 0.0).then_inc(s_l2r, 1)

                for st in range(AB_CHUNKS + 2):
                    if 1 < st < AB_CHUNKS - 1:
                        hi(b + st + 1)
                    if st == 14:
                        act.preload_act_table_set(EXP_SET)
                        act.wait_ge(s_dcl, 1)
                        for lo_, hi_ in GROUPS:
                            act.activation(eG[:, lo_:hi_, :], blocks(4 + lo_ // 4, lo_, hi_), ACT.Exp).then_inc(s_dexp, 1)
                        act.activation(dmat[:, :, :], dT[:, :, :], ACT.Exp).then_inc(s_dexp, 1)
                        act.preload_act_table_set(SILU_SET)
                    if st == 9:
                        act.wait_ge(s_cent, 1)
                        act.activation(attn[:, :, 0:T], ret[:, :, :], ACT.Square).then_inc(s_rsq, 1)
                    n = st - 1
                    if 0 <= n < AB_CHUNKS:
                        what, m = AB_ROLE[n]
                        if n in AB_GATES:
                            act.wait_ge(s_evac, n + 1 - sum(x < n for x in AB_CONV))
                            g = to[what][:, 2 * m:2 * m + 2, :]
                            act.activation(g, g, ACT.Silu).then_inc(s_gsilu, 1)
                        if n in AB_CONV[:-1]:
                            q = AB_CONV.index(n)
                            act.wait_ge(s_cx, q + 1)
                            if q >= 2:
                                act.wait_ge(s_csilu, q - 1)
                            for z in range(2):
                                t = 4 * ("gq", "gk", "gv").index(what) + 2 * m + z
                                ins = act.activation(cacc[:, q % 2, z, :], qraw[:, z, :], ACT.Copy,
                                                     scale=convw[:, 36 + t:37 + t])
                            ins.then_inc(s_tap, 1)
                    n = st - 2
                    if n in AB_CONV:
                        q = AB_CONV.index(n)
                        act.wait_ge(s_conv, q + 1)
                        what, m = AB_ROLE[n]
                        act.activation(to[what][:, 2 * m:2 * m + 2, 0:T], cacc[:, q % 2, :, :], ACT.Silu).then_inc(s_csilu, 1)
                    if st == 7:
                        for t, (_, n) in enumerate(TOK):
                            act.wait_ge(s_rvT, t + 1)
                            act.activation(rv_tok[0:n, t, :], ps[0:n, 4 + t, :], ACT.Copy).then_inc(s_rvc, 1)
                    if st == 8:
                        act.wait_ge(s_pv, 1)
                        act.activation(ret[:, :, :], ps[:, 4:8, 0:T], ACT.Copy).then_inc(s_ret, 1)
                    if st == 9:
                        l2_square(0, gk, 0, 2)
                    if st == 10:
                        act.preload_act_table_set(EXP_SET)
                        act.wait_ge(s_var, 1)
                        step.done(act.activation(attn[:, :, 0:T], ps[:, 4:8, 0:T], ACT.Ln, bias=EPS, scale=1.0 / P))
                        act.activation(attn[:, :, 0:T], attn[:, :, 0:T], ACT.Exp, scale=-0.5).then_inc(s_rrt, 1)
                    if st == 11:
                        l2_root(0, 2)
                        l2_square(1, gk, 2, 2)
                        act.wait_ge(s_x, 1)
                        step.done(act.activation(small[:, 2, :], small[:, 1, :], ACT.Exp, scale=-1.0))
                        step.done(act.activation(small[:, 2, :], small[:, 2, :], ACT.Ln, bias=1.0))
                        act.activation(small[:, 3, 0:HG], alog4[:, :], ACT.Exp)
                        act.activation(small[:, 4, :].rearrange("p (t h) -> p t h", h=HG), ba[:, :, 0:HG], ACT.Exp,
                                       scale=-1.0).then_inc(s_xe, 1)
                        act.preload_act_table_set(SILU_SET)
                    if st == 15:
                        act.preload_act_table_set(EXP_SET)
                        l2_root(1, 2)
                        l2_square(2, gq, 0, 4)
                        act.preload_act_table_set(SILU_SET)
                act.preload_act_table_set(EXP_SET)
                hi(b + AB_CHUNKS)
                l2_root(2, 4)
                act.wait_ge(s_AT, 1)
                for lo_, hi_ in GROUPS:
                    act.activation(dmat[:, lo_:hi_, :], blocks(4 + lo_ // 4, lo_, hi_), ACT.Copy).then_inc(s_ATc, 1)
                split_hi(0)
                hi(b + AB_CHUNKS + 1)
                for r in range(3):
                    for g, (lo_, hi_) in enumerate(GROUPS):
                        act.wait_ge(s_round, 3 * r + g + 1)
                        for z in range(2 if r < 2 else 1):
                            src = blocks(4 * g + z, lo_, hi_) if g < 2 else ps[:, 2, z * P:(z + 1) * P]
                            ins = act.activation(PP[:, z, lo_:hi_, :], src, ACT.Copy)
                        ins.then_inc(s_P, 1)
                for m in range(3):
                    for g, (lo_, hi_) in enumerate(GROUPS[:2]):
                        act.wait_ge(s_w1, 2 * m + g + 1)
                        act.activation(w1[:, lo_:hi_, :], blocks(4 * g, lo_, hi_), ACT.Copy).then_inc(s_w1c, 1)
                for t, (lo_, hi_) in enumerate(GROUPS):
                    act.wait_ge(s_vn, t + 1)
                    act.activation(vnew[:, 0:hi_ - lo_, :], blocks(1, lo_, hi_), ACT.Copy).then_inc(s_vnc, 1)
                    act.wait_ge(s_o, t + 1)
                    act.activation(O[:, lo_:hi_, :], blocks(2, lo_, hi_), ACT.Copy).then_inc(s_oc2, 1)
                act.wait_ge(s_oc2, 3)
                act.activation(PP[:, 0, :, :], O, ACT.Square).then_inc(s_osq, 1)
                act.wait_ge(s_oss, 1)
                step.done(act.activation(r9[:, :], r9[:, :], ACT.Ln, bias=EPS, scale=1.0 / P))
                act.activation(r9[:, :], r9[:, :], ACT.Exp, scale=-0.5).then_inc(s_ort, 1)
                split_hi(1)
                out_projection(k, b + AB_CHUNKS)

            def cd(k, b):
                def stick_scores(x):
                    act.wait_ge(s_z, x + 1)
                    act.activation(zs[x][:, :, :], ps[:, 4:8, 0:SBW], ACT.Copy, scale=DH ** -0.5).then_inc(s_zc, 1)
                    act.wait_ge(s_zc, x + 1)
                    step.done(act.activation(lb[x][:, :, :], zs[x][:, :, :], ACT.Abs))
                    step.done(act.activation(lb[x][:, :, :], lb[x][:, :, :], ACT.Exp, scale=-1.0))

                def stick_exp(x):
                    act.wait_ge(s_aw, x + 1)
                    act.activation(zs[x][:, :, :], zs[x][:, :, :], ACT.Exp).then_inc(s_ae, 1)

                def stick_out(x):
                    act.wait_ge(s_so, x + 1)
                    act.activation(yT[:, 4 + 2 * x:6 + 2 * x, :], two(2), ACT.Copy).then_inc(s_soc, 1)

                def window_exps(u):
                    n, keys = unit_shape(u)
                    act.wait_ge(s_wm, u + 1)
                    for m in range(n):
                        act.activation(unit_probs(u)[:, m, :], unit_probs(u)[:, m, :], ACT.Exp,
                                       bias=wmx[:, u % 2, 0, m:m + 1], accum_out=wmx[:, u % 2, 2, m:m + 1])
                    act.activation(wmx[:, u % 2, 1, 0:n], wmx[:, u % 2, 3, 0:n], ACT.Exp).then_inc(s_we, 1)

                for st in range(1, CD_CHUNKS + 1):
                    if st > 1:
                        hi(b + st + 1)
                    if st in (3, 5):
                        stick_scores(st // 4)
                    if st in (4, 6):
                        act.activation(lb[st // 6][:, :, :], lb[st // 6][:, :, :], ACT.Ln, bias=1.0).then_inc(s_sp, 1)
                    if st == 7:
                        stick_exp(0)
                window_exps(0)
                act.wait_ge(s_vT, 1)
                act.activation(cv_tok[:, 0:2, :], ps[:, 4, 0:2 * P].rearrange("p (t c) -> p t c", c=P), ACT.Copy)
                act.activation(cv_tok[0:16, 2, :], ps[0:16, 4, 2 * P:3 * P], ACT.Copy)
                for t in range(3):
                    act.activation(sbv_tok[:, t, :], ps[:, 5 + t, :], ACT.Copy).then_inc(s_vTc, 1)
                for u in range(UNITS):
                    if u + 1 < UNITS:
                        window_exps(u + 1)
                    if u == 0:
                        stick_exp(1)
                    act.wait_ge(s_wt, u + 1)
                    if u:
                        act.wait_ge(s_wo, u)
                    if u < 3:
                        for z in range(2):
                            ins = act.activation(probsT[:, 4 * z:4 * z + 4, :], blocks(4 + z, 0, 4), ACT.Copy)
                    else:
                        act.activation(probsT[:, 0:4, :], blocks(4, 0, 4), ACT.Copy)
                        ins = act.activation(probsT[0:16, 4:6, :], ps[0:16, 5, 0:2 * P].rearrange("p (n c) -> p n c", c=P),
                                             ACT.Copy)
                    ins.then_inc(s_wtc, 1)
                    if u == 2:
                        stick_out(0)
                    act.wait_ge(s_wo, u + 1)
                    src = ps[:, 6 + u % 2, :]
                    if u == 0:
                        act.activation(yT[:, 0:4, 0:P], blocks(6, 0, 4), ACT.Copy).then_inc(s_woc, 1)
                    elif u < 3:
                        act.activation(yT[:, 2 * u - 2:2 * u, P:2 * P], blocks(6 + u % 2, 0, 2), ACT.Copy).then_inc(s_woc, 1)
                    else:
                        act.activation(yT[:, 0:4, 2 * P:T], src[:, 0:64].rearrange("p (n c) -> p n c", c=16), ACT.Copy)\
                            .then_inc(s_woc, 1)
                act.wait_ge(s_woc, UNITS)
                act.activation(u_hi[:, 0:4, :], yT[:, 0:4, :], ACT.Copy).then_inc(s_mhi, 1)
                stick_out(1)
                act.wait_ge(s_soc, 2)
                act.activation(u_hi[:, 4:8, :], yT[:, 4:8, :], ACT.Copy).then_inc(s_mhi, 1)
                out_projection(k, b + CD_CHUNKS)

            act.preload_act_table_set(EXP_SET)
            for g in range(2):
                act.wait_ge(s_xT, 3 * g + 2)
                act.activation(hT[:, 4 * g:4 * g + 4, N_META + P:N_META + 2 * P],
                               ps[:, XB + 2 + g, :].rearrange("p (m t) -> p m t", m=4), ACT.Copy).then_inc(s_xc, 1)
                if g == 0:
                    hi(0)
            act.wait_ge(s_gains, 1)
            for k, (kind, b, layer, f) in enumerate(subs):
                hi(b + 1)
                pre_norm(k, kind, layer, b)
                if kind == "ffn":
                    act.preload_act_table_set(SILU_SET)
                    silu(f, 0)
                    with act.Fori(0, (NPAIR - 3) // 2) as i:
                        for s in (1, 2):
                            hi(b + 2 * s + 1, i)
                            hi(b + 2 * s + 2, i)
                            hidden_hi(f, s - 1, i)
                            silu(f, s, i)
                    for s in range(NPAIR - 2, NPAIR + NBLK):
                        hi(b + 2 * s + 1)
                        if s == NPAIR:
                            hidden_hi(f, s - 1)
                            act.preload_act_table_set(EXP_SET)
                        if s > NPAIR:
                            y_block(k, s - NPAIR - 1, b + 2 * s - 1)
                        hi(b + 2 * s + 2)
                        if s < NPAIR:
                            hidden_hi(f, s - 1)
                            silu(f, s)
                    y_block(k, NBLK - 1, b + SIZES[kind] - 1)
                elif kind == "ab":
                    ab(k, b)
                else:
                    cd(k, b)
                post_norm(k, kind)
            for g in range(2):
                act.wait_ge(s_oT, 2 * g + 1)
                act.activation(o_tok[:, 0, g * BANK:(g + 1) * BANK], ps[:, 2 + g, :], ACT.Copy).then_inc(s_oa, 1)

        @block.vector
        def _(dve):
            step = Steps(dve, s_dve)
            dve.sem_inc(s_lo, NRAW)
            dve.sem_inc(s_hid, 2)
            dve.sem_inc(s_prod, 2)

            def lo(n, i=0):
                if n >= n_chunks:
                    return
                if n in [b + 2 for _, b, _, _ in subs]:
                    dve.wait_ge(s_lo, NRAW + n)
                dve.wait_ge(s_hi, n + 1 + i * 4)
                src, dst = raw[:, n % NRAW, 0:rows(n) * CB], w_lo[:, n % NW, 0:rows(n) * CB]
                dve.tensor_tensor(dst, src, w_hi[:, n % NW, 0:rows(n) * CB].bitcast(F32), ALU.subtract)\
                    .then_inc(s_lo, 1)

            def scale_gate(b, f, j, i=0):
                dve.wait_ge(s_used, NW + b + 2 * j + 1 + i * 4)
                dve.wait_ge(s_prod, NPAIR * f + j + 1 + i * 2)
                tok = ffn_tokens[f]
                dve.tensor_tensor(gates[:, j % 2, :, tok], two(pair_banks(j), tok), rstd_two(1, tok), ALU.mult)\
                    .then_inc(s_gs, 1)

            def product(b, f, j, i=0):
                dve.wait_ge(s_used, NW + b + 2 * j + 2 + i * 4)
                dve.wait_ge(s_silu, NPAIR * f + j + 1 + i * 2)
                dve.wait_ge(s_hid, NPAIR * f + j + 1 + i * 2)
                tok = ffn_tokens[f]
                to = prod[:, j % 2, :, tok]
                step.done(dve.tensor_tensor(to, gates[:, j % 2, :, tok], two(pair_banks(j) + 2, tok), ALU.mult))
                dve.tensor_tensor(to, to, rstd_two(1, tok), ALU.mult).then_inc(s_prod, 1)

            def hidden_lo(f, j, i=0):
                dve.wait_ge(s_hhi, NPAIR * f + j + 1 + i * 2)
                to, tok = bass.ds(i * 4 + 2 * j, 2), ffn_tokens[f]
                dve.tensor_tensor(hid_lo[:, to, tok], prod[:, j % 2, :, tok], hid_hi[:, to, tok].bitcast(F32), ALU.subtract)\
                    .then_inc(s_hid, 1)

            def add_squares(k, blk):
                q, tok = NBLK * k + blk, out_tokens(k)
                dve.wait_ge(s_ysq0, k + 1) if blk == NBLK - 1 else dve.wait_ge(s_ysq, q + 1)
                if blk == 0:
                    if k:
                        dve.wait_ge(s_ysum, k)
                    dve.tensor_tensor(ss[:, tok], y_sq[:, q % 2, 0, tok], y_sq[:, q % 2, 1, tok], ALU.add).then_inc(s_ss, 1)
                else:
                    dve.wait_ge(s_ss, q)
                    step.done(dve.tensor_tensor(ss[:, tok], ss[:, tok], y_sq[:, q % 2, 0, tok], ALU.add))
                    dve.wait_ge(s_ysq, q + 1)
                    dve.tensor_tensor(ss[:, tok], ss[:, tok], y_sq[:, q % 2, 1, tok], ALU.add).then_inc(s_ss, 1)

            def update_h(k, g):
                m, tok = slice(2 * g, 2 * g + 2), out_tokens(k - 1)
                if g < 2:
                    step.done(dve.tensor_tensor(yT[:, m, tok], yT[:, m, tok], rstd_two(0, tok), ALU.mult))
                else:
                    dve.wait_ge(s_yr, 2 * k - 3 + g)
                dve.tensor_tensor(hT[:, m, tok], hT[:, m, tok], yT[:, m, tok], ALU.add).then_inc(s_h, 1)

            def input_lo(k, layer, g):
                for m in (2 * g, 2 * g + 1):
                    dve.wait_ge(s_uhi, KD * k + m + 1)
                    dve.scalar_tensor_tensor(u_lo[:, m, :], hT[:, m, :], gain(layer, norm_of(k), m),
                                             u_hi[:, m, :].bitcast(F32), ALU.mult, ALU.subtract).then_inc(s_ulo, 1)

            def make_input(k, kind, layer):
                if k:
                    dve.wait_ge(s_rstd, 2 * k)
                for g in range(KD // 2 + 1):
                    if k and g < KD // 2:
                        update_h(k, g)
                    if g and k < len(subs):
                        input_lo(k, layer, g - 1)

            def split_lo(half):
                dve.wait_ge(s_mhi, half + 1)
                m = slice(4 * (half % 2), 4 * (half % 2) + 4)
                dve.tensor_tensor(u_lo[:, m, :], yT[:, m, :], u_hi[:, m, :].bitcast(F32), ALU.subtract).then_inc(s_mlo, 1)

            def out_projection(k, b):
                for blk in range(NBLK):
                    lo(b + blk + 2) if blk < 3 else None
                    add_squares(k, blk)

            def conv(n):
                q, (what, half) = AB_CONV.index(n), AB_ROLE[n]
                if q:
                    dve.wait_ge(s_conv, q)
                dve.wait_ge(s_used, NW + subs[1][1] + n + 1)
                dve.tensor_tensor(qraw[:, :, :], two(2 * (n % 2)), rstd_two(1), ALU.mult).then_inc(s_cx, 1)
                own = n == AB_CONV[-1]
                if own:
                    dve.wait_ge(s_csilu, q - 1)
                    dve.wait_ge(s_cx, q + 1)
                else:
                    dve.wait_ge(s_tap, q + 1)
                for d in range(0 if own else 1, 4):
                    for m in range(2):
                        src = qraw[:, m, :]
                        t = 4 * ("gq", "gk", "gv").index(what) + 2 * half + m
                        acc, w = cacc[:, q % 2, m, :], convw[:, (3 - d) * 12 + t:(3 - d) * 12 + t + 1]
                        ins = dve.scalar_tensor_tensor(acc[:, d:T], src[:, 0:T - d], w, acc[:, d:T], ALU.mult, ALU.add) \
                            if d else dve.tensor_scalar(acc, src[:, 0:T], w, None, ALU.mult)
                        if d == 3 and m == 1:
                            ins.then_inc(s_conv, 1)
                        elif m == 1:
                            step.done(ins)

            def ab(k, b):
                sm = [small[:, n, :].rearrange("p (t h) -> p t h", h=HG) for n in range(8)]

                def l2_norm(v, x, m, count):
                    dve.wait_ge(s_l2r, v + 1)
                    dve.tensor_tensor(x[:, m:m + count, 0:T], x[:, m:m + count, 0:T], l2r[:, 0:count, :], ALU.mult)\
                        .then_inc(s_l2, 1)

                for st in range(AB_CHUNKS + 1):
                    if st == 12:
                        dve.wait_ge(s_xe, 1)
                        step.done(dve.scalar_tensor_tensor(small[:, 5, :], small[:, 0, :], 0.0, small[:, 2, :],
                                                           ALU.max, ALU.add))
                        step.done(dve.scalar_tensor_tensor(sm[6], sm[5], -1.0,
                                                           small[:, 3, 0:HG].unsqueeze(1).to_broadcast([P, 3, HG]),
                                                           ALU.mult, ALU.mult))
                        step.done(dve.tensor_scalar(small[:, 4, :], small[:, 4, :], 1.0, None, ALU.add))
                        step.done(dve.reciprocal(small[:, 7, :], small[:, 4, :]))
                        for to, n in ((g9, 6), (beta9, 7)):
                            dve.tensor_copy(to[:, 0:8], small[:, n, 0:8])
                            step.done(dve.tensor_tensor(small[:, n, 8:12], small[:, n, 8:12], head_of[:, :], ALU.mult))
                            ins = dve.tensor_reduce(to[:, 8:9], small[:, n, 8:12], AX.X, ALU.add)
                            if to is g9:
                                step.done(ins)
                        ins.then_inc(s_g9, 1)
                    if st == 13:
                        dve.wait_ge(s_gsum, 1)
                        step.done(dve.tensor_copy(gc9[:, :], ps[:, 7, 0:9]))
                        for lo_, hi_ in GROUPS:
                            ins = dve.tensor_tensor(dmat[:, lo_:hi_, :], blocks(4 + lo_ // 4, lo_, hi_),
                                                    over(gc9[:, lo_:hi_], [P, hi_ - lo_, P]), ALU.subtract)
                        step.done(ins)
                        dve.scalar_tensor_tensor(dT[:, :, :], dmat[:, :, :], -1.0, dmat[:, :, :], ALU.mult, ALU.min)\
                            .then_inc(s_dcl, 1)
                    if 0 < st < AB_CHUNKS - 1:
                        lo(b + st + 1)
                    if st == 9:
                        dve.wait_ge(s_mean, 1)
                        dve.scalar_tensor_tensor(ret[:, :, :], ps[:, 4:8, 0:T], -1.0 / P, ret[:, :, :], ALU.mult, ALU.add)\
                            .then_inc(s_cent, 1)
                    n = st - 1
                    if n in AB_CONV:
                        conv(n)
                    if st == 1:
                        dve.wait_ge(s_const, 16 * 8)
                        for m in range(KD):
                            ins = dve.tensor_scalar(w_ba[:, m, :], w_ba[:, m, :], gain(subs[k][2], norm_of(k), m), None,
                                                    ALU.mult)
                        ins.then_inc(s_wba, 1)
                        dve.wait_ge(s_rstd, 2 * k + 1)
                    if st == 2:
                        dve.wait_ge(s_ba, 1)
                        dve.wait_ge(s_pads, 4)
                        o = ps[:, 7, 0:27].rearrange("p (t c) -> p t c", c=2 * HG + 1)
                        for h_, t in [(slice(0, P), 0), (slice(0, P), 1)] + [(slice(h * TAIL, h * TAIL + 16), 2)
                                                                             for h in range(HG)]:
                            ins = dve.tensor_scalar(ba[h_, t, :], o[h_, t, 0:2 * HG], o[h_, t, 2 * HG:2 * HG + 1], None,
                                                    ALU.mult)
                        ins.then_inc(s_bac, 1)
                    n = st - 2
                    if n in AB_ROT:
                        dve.wait_ge(s_swap, n + 1)
                        if n == 0:
                            dve.wait_ge(s_tab, 32)
                        to, m = (rq, rk)[n // 2], 2 * (n % 2)
                        cos, sin = (rope[:, z:z + 1, :].to_broadcast([P, 2, T]) for z in range(2))
                        step.done(dve.tensor_tensor(rot[:, :, :], two(4), sin, ALU.mult))
                        step.done(dve.tensor_tensor(to[:, m:m + 2, :], qraw[:, :, :], cos, ALU.mult))
                        dve.tensor_tensor(to[:, m:m + 2, :], to[:, m:m + 2, :], rot[:, :, :], ALU.add).then_inc(s_rot, 1)
                        dve.wait_ge(s_rot, n + 1)
                    n = st - 1
                    if 0 <= n < AB_CHUNKS and n not in AB_CONV:
                        what, m = AB_ROLE[n]
                        dst = qraw[:, :, :] if n in AB_ROT else {"rv": rv, "rg": rg, "gz": gz}[what][:, 2 * m:2 * m + 2, :]
                        dve.wait_ge(s_used, NW + b + n + 1)
                        dve.tensor_tensor(dst, two(2 * (n % 2)), rstd_two(1), ALU.mult).then_inc(s_evac, 1)
                    if st == 6:
                        dve.wait_ge(s_score, 1)
                        dve.tensor_tensor(attn[:, :, 0:T], ps[:, 4:8, 0:T], decay[:, :, :], ALU.mult)
                        dve.tensor_tensor(attn[:, :, T:2 * T - P], ps[:, 4:8, T:2 * T - P], decay[:, :, 0:T - P], ALU.mult)
                        dve.tensor_tensor(attn[0:16, :, 2 * T - P:2 * T - P + 16], ps[0:16, 4:8, 2 * T - P:2 * T - P + 16],
                                          decay[0:16, :, 0:16], ALU.mult).then_inc(s_attn, 1)
                    if st == 8:
                        dve.wait_ge(s_bac, 1)
                        dve.wait_ge(s_const, 16 * 8)
                        step.done(dve.tensor_tensor(sm[0], ba[:, :, HG:2 * HG],
                                                    dt4[:, :].unsqueeze(1).to_broadcast([P, 3, HG]), ALU.add))
                        dve.scalar_tensor_tensor(small[:, 1, :], small[:, 0, :], -1.0, small[:, 0, :], ALU.mult, ALU.max)\
                            .then_inc(s_x, 1)
                    if st == 11:
                        dve.wait_ge(s_cent, 1)
                        dve.wait_ge(s_gsilu, 2)
                        step.done(dve.tensor_tensor(rg[:, :, :], rg[:, :, :], ret[:, :, :], ALU.mult))
                    if st == 12:
                        l2_norm(0, gk, 0, 2)
                        dve.wait_ge(s_rrt, 1)
                        dve.tensor_tensor(yT[:, 0:4, :], rg[:, :, :], attn[:, :, 0:T], ALU.mult).then_inc(s_m32, 1)
                    if st == 15:
                        dve.wait_ge(s_dexp, 4)
                        dve.tensor_tensor(dT[:, 0:8, :], dmat[:, 0:8, :], mask(UPPER, 8), ALU.mult)
                        step.done(dve.tensor_tensor(dT[:, 8, :], dmat[:, 8, :], masks[:, UPPER32, :], ALU.mult))
                        l2_norm(1, gk, 2, 2)
                dve.wait_ge(s_kT, 1)
                for g, (lo_, hi_) in enumerate(GROUPS[:2]):
                    ins = dve.tensor_tensor(ktail[:, lo_:hi_, :], blocks(g, lo_, hi_),
                                            dT[:, lo_:hi_, P - 1:P].to_broadcast([P, 4, P]), ALU.mult)
                ins.then_inc(s_ktail, 1)
                dve.wait_ge(s_dN, 1)
                dve.wait_ge(s_kk, 1)
                for g, (lo_, hi_) in enumerate(GROUPS):
                    src = blocks(4 + g, lo_, hi_) if g < 2 else ps[:, 7, 0:P].unsqueeze(1)
                    ins = dve.tensor_tensor(dN[:, lo_:hi_, :], dN[:, lo_:hi_, :], src, ALU.mult)
                ins.then_inc(s_A, 1)
                l2_norm(2, gq, 0, 4)
                for g, (lo_, hi_) in enumerate(GROUPS):
                    n = hi_ - lo_
                    dve.wait_ge(s_ATc, g + 1)
                    step.done(dve.tensor_tensor(PP[:, 1, lo_:hi_, :], dmat[:, lo_:hi_, :], mask(DIAG16, n), ALU.mult))
                    dve.tensor_tensor(XX[:, 1, lo_:hi_, :], PP[:, 1, lo_:hi_, :],
                                      ident[:, :].unsqueeze(1).to_broadcast([P, n, P]), ALU.add).then_inc(s_X0, 1)
                dve.wait_ge(s_kk, 2)
                for g, (lo_, hi_) in enumerate(GROUPS):
                    src = blocks(g, lo_, hi_) if g < 2 else ps[:, 7, P:2 * P].unsqueeze(1)
                    ins = dve.tensor_tensor(R[:, lo_:hi_, :], src, over(beta9[:, lo_:hi_], [P, hi_ - lo_, P]), ALU.mult)
                ins.then_inc(s_R, 1)
                for g, (lo_, hi_) in enumerate(GROUPS):
                    src = blocks(2 + g, lo_, hi_) if g < 2 else ps[:, 7, 0:P].unsqueeze(1)
                    ins = dve.tensor_tensor(dT[:, lo_:hi_, :], dT[:, lo_:hi_, :], src, ALU.mult)
                ins.then_inc(s_R, 1)
                egl = small[:, 0, 0:HG]
                lo(b + AB_CHUNKS)
                split_lo(0)
                lo(b + AB_CHUNKS + 1)
                for r in range(1, 4):
                    if r == 3:
                        for g, (lo_, hi_) in enumerate(GROUPS):
                            dve.wait_ge(s_P, 6 + g + 1)
                            dve.tensor_tensor(XX[:, 0, lo_:hi_, :], PP[:, 0, lo_:hi_, :],
                                              ident[:, :].unsqueeze(1).to_broadcast([P, hi_ - lo_, P]), ALU.add)\
                                .then_inc(s_IP, 1)
                    for g, (lo_, hi_) in enumerate(GROUPS):
                        dve.wait_ge(s_round, 3 * r + g + 1)
                        src = [blocks(4 * g + 2 + z, lo_, hi_) if g < 2 else
                               ps[:, 6 if r < 3 else 0, z * P:(z + 1) * P].unsqueeze(1) for z in range(2)]
                        if r == 3 and g < 2:
                            dve.tensor_copy(XX[:, 0, lo_:hi_, :], src[0])
                        dve.tensor_tensor(XX[:, 1, lo_:hi_, :], XX[:, 1, lo_:hi_, :], src[1], ALU.add).then_inc(s_X, 1)
                dve.wait_ge(s_gdec, 1)
                for m in range(3):
                    for g, (lo_, hi_) in enumerate(GROUPS[:2]):
                        dve.wait_ge(s_ATc, 3)
                        if m:
                            dve.wait_ge(s_w1, 2 * (m - 1) + g + 1)
                        dve.tensor_tensor(off_diag[:, lo_:hi_, :], dmat[:, lo_:hi_, :], mask(MERGE + m, 4), ALU.mult)\
                            .then_inc(s_E, 1)
                    for g, (lo_, hi_) in enumerate(GROUPS[:2]):
                        dve.wait_ge(s_w2, 2 * m + g + 1)
                        dve.wait_ge(s_X, 9)
                        for z in ((0, 1) if m < 2 else (1,)):
                            ins = dve.tensor_tensor(XX[:, z, lo_:hi_, :], XX[:, z, lo_:hi_, :],
                                                    blocks(4 * g + 2 + z, lo_, hi_), ALU.subtract)
                        ins.then_inc(s_T, 1)
                for t, (lo_, hi_) in enumerate(GROUPS):
                    n = hi_ - lo_
                    if t:
                        dve.wait_ge(s_ks, t)
                        step.done(dve.tensor_tensor(vtmp[:, 0:n, :], blocks(0, lo_, hi_),
                                                    over(beta9[:, lo_:hi_], [P, n, P]), ALU.mult))
                        dve.tensor_tensor(R[:, lo_:hi_, :], R[:, lo_:hi_, :], vtmp[:, 0:n, :], ALU.subtract)\
                            .then_inc(s_rhs, 1)
                    if t == 0:
                        dve.wait_ge(s_o, 1)
                        dve.tensor_copy(S[:, :, :], blocks(3, 0, 4)).then_inc(s_S, 1)
                    if t == 1:
                        dve.wait_ge(s_o, 2)
                        step.done(dve.tensor_tensor(S[:, :, :], S[:, :, :], over(egl, [P, HG, P]), ALU.mult))
                        dve.tensor_tensor(S[:, :, :], S[:, :, :], blocks(3, 0, 4), ALU.add).then_inc(s_S, 1)
                dve.wait_ge(s_osq, 1)
                dve.tensor_reduce(r9[:, :], PP[:, 0, :, :], AX.X, ALU.add).then_inc(s_oss, 1)
                dve.wait_ge(s_ort, 1)
                dve.tensor_tensor(O, O, over(r9[:, :], [P, 9, P]), ALU.mult).then_inc(s_on, 1)
                dve.wait_ge(s_gsilu, 4)
                dve.wait_ge(s_ot, 1)
                for t, (c0, n) in enumerate(TOK):
                    src = blocks(t, 0, 4) if t < 2 else \
                        ps[:, 3, 0:P].rearrange("p (h t) -> p h t", t=TAIL)[:, :, 0:n]
                    ins = dve.scalar_tensor_tensor(yT[:, 4:8, c0:c0 + n], src, out_norm[:, :], gz[:, :, c0:c0 + n],
                                                   ALU.mult, ALU.mult)
                ins.then_inc(s_m32, 1)
                split_lo(1)
                out_projection(k, b + AB_CHUNKS)

            def cd(k, b):
                def stick_log_beta(x):
                    dve.wait_ge(s_sp, x + 1)
                    step.done(dve.scalar_tensor_tensor(lb[x][:, :, :], zs[x][:, :, :], 0.0, lb[x][:, :, :],
                                                       ALU.min, ALU.subtract))

                def stick_log_rest(x):
                    dve.wait_ge(s_cdtab, 16 * 7)
                    step.done(dve.tensor_tensor(lm[x][:, :, :], lb[x][:, :, :], zs[x][:, :, :], ALU.subtract))
                    dve.tensor_tensor(lm[x][:, :, :], lm[x][:, :, :],
                                      before[:, :].unsqueeze(1).to_broadcast([P, 4, SBW]), ALU.mult).then_inc(s_lm, 1)

                def stick_exponents(x):
                    dve.wait_ge(s_cum, x + 1)
                    dve.tensor_tensor(zs[x][:, :, :], lb[x][:, :, :], ps[:, 4:8, 0:SBW], ALU.add).then_inc(s_aw, 1)

                def window_max(u):
                    n, keys = unit_shape(u)
                    t = (0, 1, 1, 2)[u]
                    sink = (sinks8[:, 0, :], sinks8[:, 1, 0:4], sinks8[:, 1, 4:8], sinks2[:, :])[u]
                    neg_max, sink_arg = wmx[:, u % 2, 0, 0:n], wmx[:, u % 2, 3, 0:n]
                    dve.wait_ge(s_ws, u + 1)
                    if u >= 2:
                        dve.wait_ge(s_wt, u - 1)
                    for m0, src in unit_scores(u):
                        w = src.shape[1]
                        ins = dve.scalar_tensor_tensor(unit_probs(u)[:, m0:m0 + w, :], src, DH ** -0.5,
                                                       window[:, t:t + 1, 0:keys].to_broadcast([P, w, keys]),
                                                       ALU.mult, ALU.add)
                    ins.then_inc(s_wst, 1)
                    dve.wait_ge(s_wst, u + 1)
                    step.done(dve.tensor_reduce(neg_max, unit_probs(u), AX.X, ALU.max))
                    step.done(dve.tensor_tensor(neg_max, neg_max, sink, ALU.max))
                    step.done(dve.tensor_tensor(sink_arg, sink, neg_max, ALU.subtract))
                    dve.tensor_scalar(neg_max, neg_max, -1.0, None, ALU.mult).then_inc(s_wm, 1)

                def window_norm(u):
                    n, keys = unit_shape(u)
                    sink_exp, total = wmx[:, u % 2, 1, 0:n], wmx[:, u % 2, 2, 0:n]
                    dve.wait_ge(s_we, u + 1)
                    step.done(dve.tensor_tensor(total, total, sink_exp, ALU.add))
                    step.done(dve.reciprocal(total, total))
                    dve.tensor_tensor(unit_probs(u), unit_probs(u), over(total, [P, n, keys]), ALU.mult).then_inc(s_wp, 1)

                for st in range(1, CD_CHUNKS + 1):
                    if st < CD_CHUNKS:
                        lo(b + st + 1)
                    if st == 1:
                        dve.wait_ge(s_rstd, 2 * k + 1)
                    c_ = CD_ORDER[st - 1]
                    dve.wait_ge(s_used, NW + b + st)
                    bank = 2 * ((st - 1) % 2)
                    if c_ == 2:
                        for head in range(2):
                            src = slice(head * DH, (head + 1) * DH)
                            for half in range(2):
                                dve.tensor_tensor(kdup[half * DH:(half + 1) * DH, head, :], ps[src, bank, 0:T],
                                                  rstd[src, 1, :], ALU.mult)
                        ins = dve.tensor_tensor(cv[:, :], ps[:, bank + 1, 0:T], rstd[:, 1, :], ALU.mult)
                    else:
                        to, m = (cq, c_) if c_ < 2 else ((sbq, sbk, sbv)[(c_ - 3) // 2], (c_ - 3) % 2)
                        ins = dve.tensor_tensor(to[:, 2 * m:2 * m + 2, 0:T], two(bank), rstd_two(1), ALU.mult)
                    ins.then_inc(s_cdc, 1)
                    if st == 4:
                        stick_log_beta(0)
                    if st == 5:
                        stick_log_rest(0)
                    if st == 6:
                        stick_exponents(0)
                        stick_log_beta(1)
                    if st == 7:
                        stick_log_rest(1)
                step.done(dve.tensor_copy(sinks8[:, 0, :].rearrange("p (s a) -> p s a", s=2),
                                          sinks8[:, 1, :].rearrange("p (a s) -> p s a", s=2)))
                window_max(0)
                stick_exponents(1)
                lo(b + CD_CHUNKS + 1)
                for u in range(UNITS):
                    if u + 1 < UNITS:
                        window_max(u + 1)
                    window_norm(u)
                split_lo(2)
                split_lo(3)
                out_projection(k, b + CD_CHUNKS)

            dve.wait_ge(s_gT, 1)
            dve.tensor_copy(gains[:, :], ps[:, 0, 0:12 * KD]).then_inc(s_gains, 1)
            dve.wait_ge(s_cwT, 1)
            dve.tensor_copy(convw[:, :], ps[:, 1, 0:4 * 12]).then_inc(s_cwc, 1)
            dve.wait_ge(s_gains, 1)
            for g in range(2):
                dve.wait_ge(s_xT, 3 * g + 3)
                for t, (n, c0) in ((0, (P, N_META)), (2, (N_META, 0))):
                    src = ps[:, XB + 2 * t + g, 0:4 * n].rearrange("p (m t) -> p m t", m=4)
                    if t:
                        dve.wait_ge(s_xc, g + 1)
                    ins = dve.tensor_copy(hT[:, 4 * g:4 * g + 4, c0:c0 + n], src)
                ins.then_inc(s_h, 2)
            lo(0)
            for k, (kind, b, layer, f) in enumerate(subs):
                make_input(k, kind, layer)
                if kind == "ffn":
                    lo(b + 2)
                    dve.wait_ge(s_rstd, 2 * k + 1)
                    scale_gate(b, f, 0)
                    with dve.Fori(0, (NPAIR - 3) // 2) as i:
                        step.enter(i, 2)
                        for s in (1, 2):
                            lo(b + 2 * s + 1, i)
                            product(b, f, s - 1, i)
                            lo(b + 2 * s + 2, i)
                            scale_gate(b, f, s, i)
                            hidden_lo(f, s - 1, i)
                    step.leave(2, (NPAIR - 3) // 2)
                    for s in range(NPAIR - 2, NPAIR + NBLK):
                        if s == NPAIR:
                            product(b, f, s - 1)
                        lo(b + 2 * s + 1)
                        if s < NPAIR:
                            product(b, f, s - 1)
                        if s > NPAIR:
                            add_squares(k, s - NPAIR - 1)
                        if s == NPAIR:
                            hidden_lo(f, s - 1)
                        lo(b + 2 * s + 2)
                        if s < NPAIR:
                            scale_gate(b, f, s)
                            hidden_lo(f, s - 1)
                    add_squares(k, NBLK - 1)
                elif kind == "ab":
                    ab(k, b)
                else:
                    cd(k, b)
            make_input(len(subs), "none", 0)
            for g in range(2):
                dve.wait_ge(s_oT, 2 * g + 2)
                dve.tensor_copy(o_tok[:, 1, g * BANK:(g + 1) * BANK], ps[:, 4 + g, :]).then_inc(s_oc, 1)

        @block.tensor
        def _(pe):
            pe.sem_inc(s_used, NW)

            def tiles(n, bank, rhs_hi, rhs_lo, i=0, first=True, last=True, final=False, between=None,
                      tok=slice(0, T)):
                pe.wait_ge(s_lo, NRAW + n + 1 + i * 4)
                for m in range(2):
                    for kk in range(rows(n)):
                        w = slice(kk * CB + m * P, kk * CB + m * P + P)
                        wh, wl = w_hi[:, n % NW, w], w_lo[:, n % NW, w]
                        o = ps[:, bank + m, tok]
                        pe.matmul(o, wh, rhs_hi[:, kk, tok], start=first and kk == 0, stop=False)
                        pe.matmul(o, wh, rhs_lo[:, kk, tok], start=False, stop=False)
                        ins = pe.matmul(o, wl, rhs_hi[:, kk, tok], start=False, stop=last and kk == rows(n) - 1)
                    if final and m == 0:
                        ins.then_inc(s_ytile, 1)
                    if between and m == 0:
                        between()
                ins.then_inc(s_used, 1)

            def first_tiles(k, n, bank):
                pe.wait_ge(s_lo, NRAW + n + 1)
                for g in range(KD // 2 + 1):
                    for lo_pass, g_ in ((False, g), (True, g - 1)):
                        if not 0 <= g_ < KD // 2:
                            continue
                        for kk in (2 * g_, 2 * g_ + 1):
                            pe.wait_ge(s_ulo if lo_pass else s_uhi, KD * k + kk + 1)
                            for m in range(2):
                                w = slice(kk * CB + m * P, kk * CB + m * P + P)
                                wh, wl = w_hi[:, n % NW, w], w_lo[:, n % NW, w]
                                tok = tokens(k)
                                o = ps[:, bank + m, tok]
                                if lo_pass:
                                    ins = pe.matmul(o, wh, u_lo[:, kk, tok], start=False, stop=kk == KD - 1,
                                                    skip_group_check=True)
                                else:
                                    pe.matmul(o, wh, u_hi[:, kk, tok], start=kk == 0, stop=False, skip_group_check=True)
                                    pe.matmul(o, wl, u_hi[:, kk, tok], start=False, stop=False, skip_group_check=True)
                ins.then_inc(s_used, 1)

            def pair(b, f, j, i=0):
                pe.wait_ge(s_prod, NPAIR * f + j + 1 + i * 2)
                tiles(b + 2 * j, pair_banks(j), u_hi, u_lo, i, tok=ffn_tokens[f])
                tiles(b + 2 * j + 1, pair_banks(j) + 2, u_hi, u_lo, i, tok=ffn_tokens[f])

            def pre_norm_sum(k, kind):
                o = ps[:, sum_bank(kind), 0:T]
                pe.wait_ge(s_hadd, k + 1)
                pe.matmul(o, ones[:, :], h_sq[:, 0, 0, :], start=True, stop=True).then_inc(s_hsum, 1)

            def post_norm_sum(k):
                pe.wait_ge(s_ss, NBLK * (k + 1))
                tok = out_tokens(k)
                pe.matmul(ps[:, 0, tok], ones[:, :], ss[:, tok], start=True, stop=True).then_inc(s_ysum, 1)

            def half_tile(n, bank, m, half, tok=slice(0, T)):
                for kk in range(4 * half, 4 * half + 4):
                    w = slice(kk * CB + m * P, kk * CB + m * P + P)
                    wh, wl = w_hi[:, n % NW, w], w_lo[:, n % NW, w]
                    for w_, u_ in ((wh, u_hi), (wh, u_lo), (wl, u_hi)):
                        ins = pe.matmul(ps[:, bank + m, tok], w_, u_[:, kk, tok], start=kk == 0 and w_ is wh and u_ is u_hi,
                                        stop=kk == KD - 1 and w_ is wl, skip_group_check=True)
                return ins

            def mm(o, lhsT, rhs, start=True, stop=True):
                return pe.matmul(o, lhsT, rhs, start=start, stop=stop, skip_group_check=True)

            def ab(k, b):
                def feat(x, q):
                    return x[:, q % 4, q // 4 * P:(q // 4 + 1) * P]

                def tails(bank, c0, x, rhs):
                    for h in range(HG):
                        ins = mm(ps[h * TAIL:(h + 1) * TAIL, bank, c0:c0 + P], x[:, h, 2 * P:TP], rhs(h))
                    return ins

                def l2_sum(v, count):
                    pe.wait_ge(s_l2sq, v + 1)
                    for m in range(count):
                        ins = mm(ps[:, m if v == 2 else 4 + m, 0:T], ones[:, :], l2sq[:, m, :])
                    ins.then_inc(s_l2sum, 1)

                for n in range(AB_CHUNKS):
                    if n >= 2:
                        if n - 2 in AB_CONV:
                            pe.wait_ge(s_cx, AB_CONV.index(n - 2) + 1)
                        else:
                            pe.wait_ge(s_evac, n - 1 - sum(x < n - 2 for x in AB_CONV))
                    if n == 0:
                        first_tiles(k, b, 0)
                    else:
                        tiles(b + n, 2 * (n % 2), u_hi, u_lo,
                              between=(lambda: pre_norm_sum(k, "ab")) if n == 1 else None)
                    if n == 1:
                        pe.wait_ge(s_wba, 1)
                        pe.wait_ge(s_rstd, 2 * k + 1)
                        for t, (c0, w) in enumerate(TOK):
                            for h in range(HG if t == 2 else 1):
                                h_ = slice(h * TAIL, h * TAIL + w)
                                for kk in range(KD):
                                    mm(ps[h_, 7, 9 * t:9 * t + 8], hT[:, kk, c0:c0 + w], w_ba[:, kk, :],
                                       kk == 0, kk == KD - 1)
                                ins = mm(ps[h_, 7, 9 * t + 8:9 * t + 9], rstd[:, 1, c0:c0 + w], ident[:, 0:1])
                        ins.then_inc(s_ba, 1)
                    if n - 1 in AB_ROT:
                        pe.wait_ge(s_evac, n)
                        if n > 1:
                            pe.wait_ge(s_rot, n - 1)
                        for m in range(2):
                            ins = mm(ps[:, 4 + m, 0:T], swap[:, :], qraw[:, m, :])
                        ins.then_inc(s_swap, 1)
                    if n == 5:
                        pe.wait_ge(s_rot, 4)
                        pe.wait_ge(s_bac, 1)
                        off = 0
                        for t, (c0, w) in enumerate(TOK):
                            for h in range(HR):
                                ins = mm(ps[0:w, 4 + h, off:off + T - c0], rk[:, h, c0:c0 + w], rq[:, h, c0:T])
                            off += T - c0
                        ins.then_inc(s_score, 1)
                    if n == 6:
                        pe.wait_ge(s_attn, 1)
                        pe.wait_ge(s_evac, 6)
                        for t, (c0, w) in enumerate(TOK):
                            for h in range(HR):
                                ins = pe.transpose(ps[0:w, 4 + t, h * P:(h + 1) * P], rv[:, h, c0:c0 + w], ident[:, :])
                            ins.then_inc(s_rvT, 1)
                    if n == 7:
                        pe.wait_ge(s_rvc, 3)
                        for h in range(HR):
                            off = 0
                            for t, (c0, w) in enumerate(TOK):
                                ins = mm(ps[:, 4 + h, c0:T], rv_tok[0:w, t, h * P:(h + 1) * P],
                                         attn[0:w, h, off:off + T - c0], t == 0, t == 2)
                                off += T - c0
                        ins.then_inc(s_pv, 1)
                    if n == 8:
                        pe.wait_ge(s_ret, 1)
                        for h in range(HR):
                            ins = mm(ps[:, 4 + h, 0:T], ones[:, :], ret[:, h, :])
                        ins.then_inc(s_mean, 1)
                    if n == 9:
                        pe.wait_ge(s_rsq, 1)
                        for h in range(HR):
                            ins = mm(ps[:, 4 + h, 0:T], ones[:, :], attn[:, h, 0:T])
                        ins.then_inc(s_var, 1)
                    if n == 10:
                        pe.wait_ge(s_rrt, 1)
                        l2_sum(0, 2)
                    if n == 14:
                        pe.wait_ge(s_dexp, 3)
                        l2_sum(1, 2)
                    if n == 12:
                        pe.wait_ge(s_l2r, 1)
                        pe.wait_ge(s_g9, 1)
                        mm(ps[:, 7, 0:8], masks[:, UPPER, :], g9[:, 0:8])
                        mm(ps[:, 7, 8:9], masks[:, UPPER32, :], g9[:, 8:9])
                        for q in range(9):
                            ins = mm(ps[:, 4 + q // 4, q % 4 * P:(q % 4 + 1) * P], g9[:, q:q + 1].to_broadcast([P, P]),
                                     masks[:, UPPER if q < 8 else UPPER32, :])
                        ins.then_inc(s_gsum, 1)
                pe.wait_ge(s_l2, 2)
                pe.wait_ge(s_pads, 4)
                pe.wait_ge(s_cx, 5)
                for q in range(8):
                    ins = pe.transpose(ps[:, q // 4, q % 4 * P:(q % 4 + 1) * P], feat(gk, q), ident[:, :])
                ins.then_inc(s_kT, 1)
                for q in range(8):
                    mm(ps[:, 4 + q // 4, q % 4 * P:(q % 4 + 1) * P], feat(gk, q), feat(gk, q))
                tails(7, 0, gk, lambda h: gk[:, :, 2 * P:TP]).then_inc(s_kk, 1)
                pe.wait_ge(s_cx, 6)
                pe.wait_ge(s_ktail, 1)
                l2_sum(2, 4)
                pe.wait_ge(s_A, 1)
                for q in range(9):
                    ins = pe.transpose(ps[:, 4 + q // 4, q % 4 * P:(q % 4 + 1) * P], dN[:, q, :], ident[:, :])
                ins.then_inc(s_AT, 1)
                pe.wait_ge(s_csilu, 6)
                pe.wait_ge(s_l2r, 3)
                for q in range(8):
                    pe.transpose(ps[:, q // 4, q % 4 * P:(q % 4 + 1) * P], feat(gv, q), ident[:, :])
                tails(7, P, gv, lambda h: ident[:, :])
                pe.wait_ge(s_l2, 3)
                for q in range(8):
                    mm(ps[:, 2 + q // 4, q % 4 * P:(q % 4 + 1) * P], feat(gk, q), feat(gq, q))
                tails(7, 0, gk, lambda h: gq[:, :, 2 * P:TP]).then_inc(s_kk, 1)
                for r in range(4):
                    for g, (lo_, hi_) in enumerate(GROUPS):
                        if r == 0:
                            pe.wait_ge(s_X0, g + 1)
                            pe.wait_ge(s_PP0, 1)
                            pe.wait_ge(s_R, 1 + (g > 0))
                            if g == 1:
                                pe.wait_ge(s_X0, 3)
                                pe.wait_ge(s_ATc, 3)
                        else:
                            pe.wait_ge(s_P, 3 * r - 2 + g)
                            if r > 1:
                                pe.wait_ge(s_X, 3 * r - 5 + g)
                        for q in range(lo_, hi_):
                            def o(z):
                                return ps[:, 4 * g + z, (q - lo_) * P:(q - lo_ + 1) * P] if g < 2 else \
                                    ps[:, (2 if z < 2 else 6) if r < 3 else 0, z % 2 * P:(z % 2 + 1) * P]
                            p_, pt, xt = PP[:, 0, q, :], PP[:, 1, q, :], XX[:, 1, q, :]
                            if r < 3:
                                ins = mm(o(0), pt, p_)
                            if r < 2:
                                ins = mm(o(1), p_, pt)
                            if r:
                                ins = mm(o(3), p_, xt)
                        if r == 3 and g < 2:
                            pe.wait_ge(s_IP, g + 1)
                            pe.wait_ge(s_P, 9)
                            pe.wait_ge(s_X, 6)
                            for q in range(lo_, hi_):
                                ins = mm(ps[:, 4 * g + 2, (q - lo_) * P:(q - lo_ + 1) * P], XX[:, 1, q, :], XX[:, 0, q, :])
                        ins.then_inc(s_round, 1)
                for m in range(3):
                    for g, (lo_, hi_) in enumerate(GROUPS[:2]):
                        pe.wait_ge(s_E, 2 * m + g + 1)
                        pe.wait_ge(s_X, 9)
                        if m:
                            pe.wait_ge(s_T, 2 * (m - 1) + g + 1)
                        for q in range(lo_, hi_):
                            ins = mm(ps[:, 4 * g, (q - lo_) * P:(q - lo_ + 1) * P], off_diag[:, q, :], XX[:, 0, q, :])
                        ins.then_inc(s_w1, 1)
                    for g, (lo_, hi_) in enumerate(GROUPS[:2]):
                        pe.wait_ge(s_w1c, 2 * m + g + 1)
                        for q in range(lo_, hi_):
                            c_ = slice((q - lo_) * P, (q - lo_ + 1) * P)
                            if m < 2:
                                mm(ps[:, 4 * g + 2, c_], XX[:, 1, q, :], w1[:, q, :])
                            ins = mm(ps[:, 4 * g + 3, c_], w1[:, q, :], XX[:, 1, q, :])
                        ins.then_inc(s_w2, 1)
                pe.wait_ge(s_T, 6)
                pe.wait_ge(s_gdec, 1)

                def retention_half(i, m):
                    pe.wait_ge(s_lo, NRAW + b + AB_CHUNKS + i + 1)
                    pe.wait_ge(s_mlo, 1)
                    half_tile(b + AB_CHUNKS + i, 2 * block_at("ab", i), m, 0)

                for t, (lo_, hi_) in enumerate(GROUPS):
                    if t:
                        pe.wait_ge(s_S, t)
                        if t == 1:
                            for h in range(HG):
                                ins = mm(ps[:, 0, h * P:(h + 1) * P], feat(gk, 4 + h), S[:, h, :])
                        else:
                            ins = tails(0, 0, gk, lambda h: S[:, h, :])
                        ins.then_inc(s_ks, 1)
                        retention_half(0, t - 1)
                        pe.wait_ge(s_rhs, t)
                        pe.wait_ge(s_vnc, t)
                    for q in range(lo_, hi_):
                        ins = mm(ps[:, 1, (q - lo_) * P:(q - lo_ + 1) * P], XX[:, 1, q, :], R[:, q, :])
                    ins.then_inc(s_vn, 1)
                    if t:
                        pe.wait_ge(s_oc2, t)
                    if t == 2:
                        tails(2, 0, gq, lambda h: S[:, h, :])
                    pe.wait_ge(s_vnc, t + 1)
                    for q in range(lo_, hi_):
                        o = ps[:, 2, (q - lo_) * P:(q - lo_ + 1) * P]
                        if t == 1:
                            mm(o, feat(gq, q), S[:, q - 4, :], True, False)
                        ins = mm(o, dT[:, q, :], vnew[:, q - lo_, :], t == 0, True)
                    if t < 2:
                        for q in range(lo_, hi_):
                            ins = mm(ps[:, 3, (q - lo_) * P:(q - lo_ + 1) * P], ktail[:, q, :], vnew[:, q - lo_, :])
                    ins.then_inc(s_o, 1)
                retention_half(1, 0)
                retention_half(1, 1)
                pe.wait_ge(s_on, 1)
                for q in range(9):
                    ins = pe.transpose(ps[:, (0, 1, 3)[q // 4], q % 4 * P:(q % 4 + 1) * P], O[:, q, :], ident[:, :])
                ins.then_inc(s_ot, 1)
                n = b + AB_CHUNKS
                pe.wait_ge(s_mlo, 2)
                for i in range(2):
                    for m in range(2):
                        ins = half_tile(n + i, 2 * block_at("ab", i), m, 1)
                    ins.then_inc(s_used, 1)
                for i in (2, 3):
                    tiles(n + i, 2 * block_at("ab", i), u_hi, u_lo, final=i == 3)

            def cd(k, b):
                def half(s):
                    return slice(s * DH, (s + 1) * DH)

                offs = [0, T, 2 * T - P]

                def stick_scores(x):
                    pe.wait_ge(s_cdc, 2 * x + 2)
                    if x:
                        pe.wait_ge(s_zc, x)
                    for h in range(4 * x, 4 * x + 4):
                        for j, (k0, q0) in enumerate(SB_TILES):
                            ins = mm(ps[:, 4 + h % 4, offs[j]:offs[j] + T - q0], sbk[half(h % 2), h // 2, k0:k0 + P],
                                     sbq[half(h % 2), h // 2, q0:T])
                    ins.then_inc(s_z, 1)

                def stick_sums(x):
                    pe.wait_ge(s_lm, x + 1)
                    pe.wait_ge(s_aw, 1) if x else pe.wait_ge(s_zc, 2)
                    for h in range(4):
                        for j, (k0, q0) in enumerate(SB_TILES):
                            for i in range(j, 3):
                                q1 = SB_TILES[i][1]
                                ins = mm(ps[:, 4 + h, offs[j] + q1 - q0:offs[j] + T - q0],
                                         masks[:, LOWER, :] if i == j else ones[:, :],
                                         lm[x][:, h, offs[i]:offs[i] + T - q1], i == j, i == 2)
                    ins.then_inc(s_cum, 1)

                def stick_out(x):
                    pe.wait_ge(s_am, x + 1)
                    if x:
                        pe.wait_ge(s_soc, x)
                    for h in range(4 * x, 4 * x + 4):
                        for j, (k0, q0) in enumerate(SB_TILES):
                            ins = mm(ps[half(h % 2), 2 + h // 2 % 2, q0:T], sbv_tok[:, j, h * DH:(h + 1) * DH],
                                     zs[x][:, h % 4, offs[j]:offs[j] + T - q0], j == 0, j == 2)
                    ins.then_inc(s_so, 1)

                def window_scores(u):
                    if u:
                        pe.wait_ge(s_wst, u)
                    for h in range(HS):
                        s_, t_ = h % 2, h // 2
                        q, kk = cq[half(s_), t_, :], kdup[half(s_), h // 4, :]
                        if u == 0:
                            ins = mm(ps[:, s_, t_ * P:(t_ + 1) * P], q[:, 0:P], kk[:, 0:P])
                        elif u == h // 4 + 1:
                            ins = mm(ps[:, h % 4, 0:2 * P], q[:, P:2 * P], kk[:, 0:2 * P])
                        elif u == 3:
                            ins = mm(ps[t_ * TAIL:(t_ + 1) * TAIL, s_, 0:T], q[:, 2 * P:TP], kk[:, 0:T])
                    ins.then_inc(s_ws, 1)

                for n in range(CD_CHUNKS):
                    if n >= 2:
                        pe.wait_ge(s_cdc, n - 1)
                    if n == 0:
                        first_tiles(k, b, 0)
                    else:
                        tiles(b + n, 2 * (n % 2), u_hi, u_lo,
                              between=(lambda: pre_norm_sum(k, "cd")) if n == 1 else None)
                    if n in (2, 4):
                        stick_scores(n // 4)
                    if n == 5:
                        stick_sums(0)
                pe.wait_ge(s_cdc, CD_CHUNKS)
                pe.wait_ge(s_cdpad, 1)
                window_scores(0)
                stick_sums(1)
                window_scores(1)
                pe.wait_ge(s_aw, 2)
                for t, (c0, n) in enumerate(TOK):
                    pe.transpose(ps[0:n, 4, t * P:(t + 1) * P], cv[:, c0:c0 + n], ident[:, :])
                for t, (k0, _) in enumerate(SB_TILES):
                    for m in range(4):
                        ins = pe.transpose(ps[:, 5 + t, m * P:(m + 1) * P], sbv[:, m, k0:k0 + P], ident[:, :])
                ins.then_inc(s_vT, 1)
                for u in range(UNITS):
                    n, keys = unit_shape(u)
                    if u + 2 < UNITS:
                        window_scores(u + 2)
                    pe.wait_ge(s_wp, u + 1)
                    pe.wait_ge(s_wtc, u) if u else pe.wait_ge(s_vTc, 3)
                    for m in range(n):
                        src = unit_probs(u)[:, m, :]
                        if u == 0:
                            ins = pe.transpose(ps[:, 4 + m // 4, m % 4 * P:(m % 4 + 1) * P], src, ident[:, :])
                        else:
                            for kt in range((keys + P - 1) // P):
                                w = min(P, keys - kt * P)
                                o = ps[0:w, 4 + kt, m * P:(m + 1) * P] if u < 3 else \
                                    ps[0:w, 4 + kt // 2, (2 * (kt % 2) + m) * P:(2 * (kt % 2) + m + 1) * P]
                                ins = pe.transpose(o, src[:, kt * P:kt * P + w], ident[:, :])
                    ins.then_inc(s_wt, 1)
                    if u == 1:
                        pe.wait_ge(s_wst, 3)
                        stick_out(0)
                    pe.wait_ge(s_wtc, u + 1)
                    if u >= 2:
                        pe.wait_ge(s_woc, u - 1)
                    for h in range(HS):
                        s_, t_, g_ = h % 2, h // 2, slice(h // 4 * DH, h // 4 * DH + DH)
                        o = ps[half(s_), 6 + u % 2, :]
                        if u == 0:
                            ins = mm(o[:, t_ * P:(t_ + 1) * P], cv_tok[:, 0, g_], probsT[:, 4 * s_ + t_, :])
                        elif u == h // 4 + 1:
                            for kt in range(2):
                                ins = mm(o[:, t_ % 2 * P:(t_ % 2 + 1) * P], cv_tok[:, kt, g_],
                                         probsT[:, 4 * kt + h % 4, :], kt == 0, kt == 1)
                        elif u == 3:
                            for kt, (_, w) in enumerate(TOK):
                                ins = mm(o[:, t_ * 16:(t_ + 1) * 16], cv_tok[0:w, kt, g_],
                                         probsT[0:w, 2 * kt + s_, t_ * TAIL:t_ * TAIL + 16], kt == 0, kt == 2)
                    ins.then_inc(s_wo, 1)
                stick_out(1)
                n = b + CD_CHUNKS
                pe.wait_ge(s_wtc, UNITS)
                for half_ in range(2):
                    pe.wait_ge(s_mlo, 3 + half_)
                    for i in range(2):
                        pe.wait_ge(s_lo, NRAW + n + i + 1)
                        for m in range(2):
                            ins = half_tile(n + i, 2 * block_at("cd", i), m, half_, out_tokens(k))
                        if half_:
                            ins.then_inc(s_used, 1)
                for i in (2, 3):
                    tiles(n + i, 2 * block_at("cd", i), u_hi, u_lo, final=i == 3, tok=out_tokens(k))

            pe.wait_ge(s_const, 16)
            pe.wait_ge(s_in, 80)
            pe.transpose(ps[:, 0, 0:12 * KD], g_tok[:, :], ident[0:12 * KD, 0:12 * KD]).then_inc(s_gT, 1)
            pe.transpose(ps[:, 1, 0:4 * 12], cw_tok[:, :], ident[0:4 * 12, 0:4 * 12]).then_inc(s_cwT, 1)
            for g in range(2):
                for t, n in enumerate((P, P, N_META)):
                    for m in range(4):
                        src = x_tok[0:n, t, (4 * g + m) * P:(4 * g + m + 1) * P]
                        ins = pe.transpose(ps[:, XB + 2 * t + g, m * n:(m + 1) * n], src, ident[0:n, 0:n])
                    ins.then_inc(s_xT, 1)
            pe.wait_ge(s_ones, 1)
            pe.wait_ge(s_cwc, 1)
            pe.wait_ge(s_h, KD // 2)
            for k, (kind, b, layer, f) in enumerate(subs):
                if kind == "ffn":
                    pe.wait_ge(s_prod, NPAIR * f + 1)
                    first_tiles(k, b, pair_banks(0))
                    tiles(b + 1, pair_banks(0) + 2, u_hi, u_lo, between=lambda: pre_norm_sum(k, kind),
                          tok=tokens(k))
                    pe.wait_ge(s_rstd, 2 * k + 1)
                    with pe.Fori(0, (NPAIR - 3) // 2) as i:
                        pair(b, f, 1, i)
                        pair(b, f, 2, i)
                    pair(b, f, NPAIR - 2)
                    pair(b, f, NPAIR - 1)
                    for blk in range(NBLK):
                        for half in range(2):
                            pe.wait_ge(s_prod, 2 + NPAIR * f + NPAIR - 1 + (blk > 0))
                            pe.wait_ge(s_hid, 2 + NPAIR * f + (NPAIR if half else (KH + 1) // 2))
                            h = slice(half * KH, (half + 1) * KH)
                            tiles(b + 2 * NPAIR + 2 * blk + half, 2 * blk, hid_hi[:, h, :], hid_lo[:, h, :],
                                  first=half == 0, last=half == 1, final=blk == NBLK - 1 and half == 1, tok=tokens(k))
                elif kind == "ab":
                    ab(k, b)
                else:
                    cd(k, b)
                post_norm_sum(k)
            for g in range(2):
                for t in range(2):
                    pe.wait_ge(s_h, KD // 2 * len(subs) + 2 * g + 2)
                    for m in range(4):
                        src = hT[:, 4 * g + m, N_META + t * P:N_META + (t + 1) * P]
                        ins = pe.transpose(ps[:, 2 + 2 * t + g, m * P:(m + 1) * P], src, ident[:, :])
                    ins.then_inc(s_oT, 1)


INPUTS = ["x", "meta_tokens", "norm_gains", "ffn_w_gate", "ffn_w_up", "ffn_w_down", "ab_w_in", "ab_conv_w",
          "ab_a_log", "ab_dt_bias", "ab_out_norm", "ab_w_out", "cd_w_in", "cd_sinks", "cd_w_out"]


def kernel(**inputs):
    import concourse.bacc as bacc
    from concourse.bass_utils import run_bass_kernel_spmd

    nc = bacc.Bacc("TRN2", target_bir_lowering=False, num_devices=1)
    tables = shape_constants()
    arrays = {name: np.ascontiguousarray(inputs[name]) for name in INPUTS} | tables
    aps = {name: nc.dram_tensor(name, v.shape, mybir.dt.from_np(v.dtype), kind="ExternalInput").ap()
           for name, v in arrays.items()}
    out = nc.dram_tensor("out", (1, SEQ, D), F32, kind="ExternalOutput").ap()
    build(nc, aps, {name: aps[name] for name in tables}, out)
    return run_bass_kernel_spmd(nc, [arrays], core_ids=[0]).results[0]["out"]
```
